# Optimizing a Trainium2 kernel written in Bass

```python
import math
import jax
import jax.numpy as jnp
from jax import lax
import numpy as np

D_MODEL = 2048
BATCH = 1
SEQ = 256
DEPTH = 1

CTX_LEN = 256
GRID_W = 64
EPS = 1e-6
F32 = jnp.float32

S5_WIDTH = D_MODEL // 2
S5_GROUP = 16
S5_GROUPS = S5_WIDTH // S5_GROUP
S5_STATE = 64
SCAN_CHUNK = 128

LRU_WIDTH = D_MODEL // 2
LRU_HEADS = 16
LRU_BLOCK = LRU_WIDTH // LRU_HEADS
LRU_C = 8.0
CONV_W = 4
CONV_PAD_LO = (CONV_W - 1) // 2
CONV_PAD_HI = CONV_W - 1 - CONV_PAD_LO

N_KEYS = 128
N_EXPERTS = N_KEYS * N_KEYS
PEER_HEADS = 8
PEER_TOPK = 16
PEER_DKEY = 256
PEER_HALF = PEER_DKEY // 2
TOKEN_BLOCK = 128

IN_WIDTH = S5_WIDTH + 2 * LRU_WIDTH + 2 * D_MODEL

kernel_name = 'hybrid_s5_rglru_peer_dit'

def rmsnorm(t, g):
    tf = t.astype(F32)
    y = tf * lax.rsqrt(jnp.mean(tf * tf, axis=-1, keepdims=True) + EPS)
    return (y * g.astype(F32)).astype(t.dtype)

def modulate(t, shift, scale):
    return t * (1 + scale) + shift

def flip_seq(t, rev):
    return jnp.flip(t, axis=1) if rev else t

def linear_combine(e1, e2):
    a1, b1 = e1
    a2, b2 = e2
    return a1 * a2, a2 * b1 + b2

def to_colmajor(t, rows):
    bsz, _, w = t.shape
    return t.reshape(bsz, rows, GRID_W, w).transpose(0, 2, 1, 3)

def from_colmajor(t):
    bsz, gw, rows, w = t.shape
    return t.transpose(0, 2, 1, 3).reshape(bsz, rows * gw, w)

def dwconv(t, w, b):
    out = lax.conv_general_dilated(t, w[:, None, :], window_strides=(1,),
                                   padding=[(CONV_PAD_LO, CONV_PAD_HI)],
                                   dimension_numbers=('NWC', 'WIO', 'NWC'),
                                   feature_group_count=t.shape[-1])
    return out + b

def s5_scan(u, h0, a_bar, b_bar, c_mat, with_output):
    bsz, length = u.shape[0], u.shape[1]
    n_chunks = length // SCAN_CHUNK
    u_chunks = u.reshape(bsz, n_chunks, SCAN_CHUNK, S5_GROUPS, S5_GROUP).swapaxes(0, 1)
    a_seq = jnp.broadcast_to(a_bar, (bsz, SCAN_CHUNK, S5_GROUPS, S5_STATE))

    def step(h, u_blk):
        bu = jnp.einsum('btgh,gph->btgp', u_blk.astype(jnp.complex64), b_bar)
        bu = bu.at[:, 0].add(a_bar * h)
        _, hs = lax.associative_scan(linear_combine, (a_seq, bu), axis=1)
        y = jnp.einsum('btgp,ghp->btgh', hs, c_mat).real if with_output else None
        return hs[:, -1], y

    h_last, y = lax.scan(step, h0, u_chunks)
    if with_output:
        y = y.swapaxes(0, 1).reshape(bsz, length, S5_GROUPS, S5_GROUP)
    return y, h_last

def s5_mixer(u_lat, u_ctx, need_ctx, a_re, a_im, log_dt, b_re, b_im, c_re, c_im, d_skip, w_glu):
    dtype = u_lat.dtype
    bsz = u_lat.shape[0]
    ul = u_lat.astype(F32).reshape(bsz, -1, S5_GROUPS, S5_GROUP)
    uc = u_ctx.astype(F32).reshape(bsz, -1, S5_GROUPS, S5_GROUP)
    d_g = d_skip.astype(F32).reshape(S5_GROUPS, S5_GROUP)
    y_lat = d_g * ul
    y_ctx = d_g * uc if need_ctx else None
    for d in range(2):
        rev = d == 1
        lam = lax.complex(a_re[d].astype(F32), a_im[d].astype(F32))
        dt = jnp.exp(log_dt[d].astype(F32))[:, None]
        a_bar = jnp.exp(lam * dt)
        b_bar = ((a_bar - 1.0) / lam)[..., None] * lax.complex(b_re[d].astype(F32), b_im[d].astype(F32))
        c_mat = lax.complex(c_re[d].astype(F32), c_im[d].astype(F32))
        h0 = jnp.zeros((bsz, S5_GROUPS, S5_STATE), jnp.complex64)
        yc, hc = s5_scan(flip_seq(uc, rev), h0, a_bar, b_bar, c_mat, need_ctx)
        yl, _ = s5_scan(flip_seq(ul, rev), hc, a_bar, b_bar, c_mat, True)
        y_lat = y_lat + flip_seq(yl, rev)
        if need_ctx:
            y_ctx = y_ctx + flip_seq(yc, rev)

    def glu(y):
        z = jax.nn.gelu(y.reshape(y.shape[0], y.shape[1], S5_WIDTH).astype(dtype))
        return z * jax.nn.sigmoid(z @ w_glu)

    return glu(y_lat), (glu(y_ctx) if need_ctx else None)

def rglru_scan(x, h0, lam, w_r, b_r, w_i, b_i):
    xb = x.reshape(x.shape[0], x.shape[1], LRU_HEADS, LRU_BLOCK)
    r = jax.nn.sigmoid(jnp.einsum('blhi,hij->blhj', xb, w_r.astype(F32)).reshape(x.shape) + b_r.astype(F32))
    i = jax.nn.sigmoid(jnp.einsum('blhi,hij->blhj', xb, w_i.astype(F32)).reshape(x.shape) + b_i.astype(F32))
    log_a = -LRU_C * r * jax.nn.softplus(-lam.astype(F32))
    a = jnp.exp(log_a)
    bx = jnp.sqrt(-jnp.expm1(2.0 * log_a)) * (i * x)
    bx = bx.at[:, 0].add(a[:, 0] * h0)
    _, h = lax.associative_scan(linear_combine, (a, bx), axis=1)
    return h, h[:, -1]

def lru_mixer(v_lat, v_ctx, rows, need_ctx, conv_w, conv_b, lam, w_r, b_r, w_i, b_i):
    dtype = v_lat.dtype
    bsz, length, width = v_lat.shape
    vl = to_colmajor(v_lat, rows).reshape(bsz * GRID_W, rows, width)
    xl = dwconv(vl, conv_w, conv_b).reshape(bsz, length, width).astype(F32)
    xc = dwconv(v_ctx, conv_w, conv_b).astype(F32)
    ys_lat = []
    ys_ctx = []
    for d in range(2):
        rev = d == 1
        h0 = jnp.zeros((bsz, width), F32)
        hc, hc_last = rglru_scan(flip_seq(xc, rev), h0, lam[d], w_r[d], b_r[d], w_i[d], b_i[d])
        hl, _ = rglru_scan(flip_seq(xl, rev), hc_last, lam[d], w_r[d], b_r[d], w_i[d], b_i[d])
        ys_lat.append(flip_seq(hl, rev))
        if need_ctx:
            ys_ctx.append(flip_seq(hc, rev))
    y_lat = from_colmajor((ys_lat[0] + ys_lat[1]).reshape(bsz, GRID_W, rows, width))
    y_ctx = (ys_ctx[0] + ys_ctx[1]).astype(dtype) if need_ctx else None
    return y_lat.astype(dtype), y_ctx

def mixer_block(n_lat, n_ctx, rows, need_ctx, w_in, s5_a_re, s5_a_im, s5_log_dt, s5_b_re, s5_b_im,
                s5_c_re, s5_c_im, s5_d, s5_w_glu, lru_conv_w, lru_conv_b, lru_lambda, lru_w_r, lru_b_r,
                lru_w_i, lru_b_i, w_proj_a, w_proj_b, w_out):
    o_v = S5_WIDTH
    o_g = o_v + LRU_WIDTH
    o_ga = o_g + LRU_WIDTH
    o_gb = o_ga + D_MODEL
    z_lat = n_lat @ w_in
    z_ctx = n_ctx @ (w_in if need_ctx else w_in[:, :o_g])
    ya_lat, ya_ctx = s5_mixer(z_lat[..., :o_v], z_ctx[..., :o_v], need_ctx, s5_a_re, s5_a_im, s5_log_dt,
                              s5_b_re, s5_b_im, s5_c_re, s5_c_im, s5_d, s5_w_glu)
    yb_lat, yb_ctx = lru_mixer(z_lat[..., o_v:o_g], z_ctx[..., o_v:o_g], rows, need_ctx, lru_conv_w,
                               lru_conv_b, lru_lambda, lru_w_r, lru_b_r, lru_w_i, lru_b_i)

    def merge(z, ya, yb):
        yb = yb * jax.nn.gelu(z[..., o_g:o_ga])
        m = jax.nn.sigmoid(z[..., o_ga:o_gb]) * (ya @ w_proj_a) + jax.nn.sigmoid(z[..., o_gb:]) * (yb @ w_proj_b)
        return m @ w_out

    out_lat = merge(z_lat, ya_lat, yb_lat)
    out_ctx = merge(z_ctx, ya_ctx, yb_ctx) if need_ctx else None
    return out_lat, out_ctx

def peer_ffn(t, w_query, sub_keys, expert_u, expert_v):
    shape = t.shape
    tokens = t.reshape(-1, TOKEN_BLOCK, D_MODEL)
    sk = sub_keys.astype(F32)
    kk = PEER_TOPK * PEER_TOPK

    def block(xb):
        q = (xb @ w_query).astype(F32).reshape(TOKEN_BLOCK, PEER_HEADS, 2, PEER_HALF)
        s = jnp.einsum('thsc,snc->thsn', q, sk)
        sv, si = lax.top_k(s, PEER_TOPK)
        cand = (sv[:, :, 0, :, None] + sv[:, :, 1, None, :]).reshape(TOKEN_BLOCK, PEER_HEADS, kk)
        cand_idx = (si[:, :, 0, :, None] * N_KEYS + si[:, :, 1, None, :]).reshape(TOKEN_BLOCK, PEER_HEADS, kk)
        top_s, top_pos = lax.top_k(cand, PEER_TOPK)
        e_idx = jnp.take_along_axis(cand_idx, top_pos, axis=-1)
        g = jax.nn.softmax(top_s, axis=-1)
        u = expert_u[e_idx]
        v = expert_v[e_idx]
        act = jax.nn.gelu(jnp.einsum('td,thkd->thk', xb, u).astype(F32))
        return jnp.einsum('thk,thkd->td', (g * act).astype(t.dtype), v)

    return lax.map(block, tokens).reshape(shape)

def setup_inputs(seed: int = 0) -> dict:
    key = jax.random.key(seed)
    k = jax.random.split(key, 40)

    def nrm(i, shape, scale):
        return jax.random.normal(k[i], shape, F32) * scale

    lam_im = jnp.broadcast_to(math.pi * jnp.arange(S5_STATE, dtype=F32), (DEPTH, 2, S5_GROUPS, S5_STATE))
    a_pow = jax.random.uniform(k[20], (DEPTH, 2, LRU_WIDTH), F32, minval=0.9, maxval=0.999)
    a_base = a_pow ** (1.0 / LRU_C)
    return {
        'x': nrm(0, (BATCH, SEQ, D_MODEL), 1.0),
        'c': nrm(1, (BATCH, D_MODEL), 1.0),
        'ctx': nrm(2, (BATCH, CTX_LEN, D_MODEL), 1.0),
        'c_ctx': nrm(3, (D_MODEL,), 1.0),
        'w_ada': nrm(4, (DEPTH, D_MODEL, 6 * D_MODEL), 0.5 * D_MODEL ** -0.5),
        'b_ada': nrm(5, (DEPTH, 6 * D_MODEL), 0.01),
        'g_norm1': 1.0 + nrm(6, (DEPTH, D_MODEL), 0.02),
        'w_in': nrm(7, (DEPTH, D_MODEL, IN_WIDTH), D_MODEL ** -0.5),
        's5_a_re': -0.5 + nrm(8, (DEPTH, 2, S5_GROUPS, S5_STATE), 0.01),
        's5_a_im': lam_im + nrm(9, (DEPTH, 2, S5_GROUPS, S5_STATE), 0.01),
        's5_log_dt': jax.random.uniform(k[10], (DEPTH, 2, S5_GROUPS), F32, minval=math.log(0.001), maxval=math.log(0.1)),
        's5_b_re': nrm(11, (DEPTH, 2, S5_GROUPS, S5_STATE, S5_GROUP), (2 * S5_GROUP) ** -0.5),
        's5_b_im': nrm(12, (DEPTH, 2, S5_GROUPS, S5_STATE, S5_GROUP), (2 * S5_GROUP) ** -0.5),
        's5_c_re': nrm(13, (DEPTH, 2, S5_GROUPS, S5_GROUP, S5_STATE), (2 * S5_STATE) ** -0.5),
        's5_c_im': nrm(14, (DEPTH, 2, S5_GROUPS, S5_GROUP, S5_STATE), (2 * S5_STATE) ** -0.5),
        's5_d': nrm(15, (DEPTH, S5_WIDTH), 1.0),
        's5_w_glu': nrm(16, (DEPTH, S5_WIDTH, S5_WIDTH), S5_WIDTH ** -0.5),
        'lru_conv_w': nrm(17, (DEPTH, CONV_W, LRU_WIDTH), CONV_W ** -0.5),
        'lru_conv_b': nrm(18, (DEPTH, LRU_WIDTH), 0.01),
        'lru_lambda': jnp.log(a_base) - jnp.log1p(-a_base),
        'lru_w_r': nrm(21, (DEPTH, 2, LRU_HEADS, LRU_BLOCK, LRU_BLOCK), LRU_BLOCK ** -0.5),
        'lru_b_r': nrm(22, (DEPTH, 2, LRU_WIDTH), 0.01),
        'lru_w_i': nrm(23, (DEPTH, 2, LRU_HEADS, LRU_BLOCK, LRU_BLOCK), LRU_BLOCK ** -0.5),
        'lru_b_i': nrm(24, (DEPTH, 2, LRU_WIDTH), 0.01),
        'w_proj_a': nrm(25, (DEPTH, S5_WIDTH, D_MODEL), S5_WIDTH ** -0.5),
        'w_proj_b': nrm(26, (DEPTH, LRU_WIDTH, D_MODEL), LRU_WIDTH ** -0.5),
        'w_out': nrm(27, (DEPTH, D_MODEL, D_MODEL), D_MODEL ** -0.5),
        'g_norm2': 1.0 + nrm(28, (DEPTH, D_MODEL), 0.02),
        'peer_w_query': nrm(29, (DEPTH, D_MODEL, PEER_HEADS * PEER_DKEY), D_MODEL ** -0.5),
        'peer_sub_keys': nrm(30, (DEPTH, 2, N_KEYS, PEER_HALF), PEER_HALF ** -0.5),
        'peer_u': nrm(31, (DEPTH, N_EXPERTS, D_MODEL), D_MODEL ** -0.5),
        'peer_v': nrm(32, (DEPTH, N_EXPERTS, D_MODEL), PEER_HEADS ** -0.5),
        'g_final': 1.0 + nrm(33, (D_MODEL,), 0.02),
    }

def reference(x, c, ctx, c_ctx, w_ada, b_ada, g_norm1, w_in, s5_a_re, s5_a_im, s5_log_dt, s5_b_re,
              s5_b_im, s5_c_re, s5_c_im, s5_d, s5_w_glu, lru_conv_w, lru_conv_b, lru_lambda, lru_w_r,
              lru_b_r, lru_w_i, lru_b_i, w_proj_a, w_proj_b, w_out, g_norm2, peer_w_query, peer_sub_keys,
              peer_u, peer_v, g_final):
    rows = x.shape[1] // GRID_W
    sc_lat = jax.nn.silu(c)
    sc_ctx = jax.nn.silu(c_ctx)
    h_lat = x
    h_ctx = ctx
    for layer in range(DEPTH):
        need_ctx = layer < DEPTH - 1
        mod_l = jnp.split((sc_lat @ w_ada[layer] + b_ada[layer])[:, None, :], 6, axis=-1)
        mod_c = jnp.split((sc_ctx @ w_ada[layer] + b_ada[layer])[None, None, :], 6, axis=-1)

        n_lat = modulate(rmsnorm(h_lat, g_norm1[layer]), mod_l[0], mod_l[1])
        n_ctx = modulate(rmsnorm(h_ctx, g_norm1[layer]), mod_c[0], mod_c[1])
        mix_lat, mix_ctx = mixer_block(
            n_lat, n_ctx, rows, need_ctx, w_in[layer], s5_a_re[layer], s5_a_im[layer], s5_log_dt[layer],
            s5_b_re[layer], s5_b_im[layer], s5_c_re[layer], s5_c_im[layer], s5_d[layer], s5_w_glu[layer],
            lru_conv_w[layer], lru_conv_b[layer], lru_lambda[layer], lru_w_r[layer], lru_b_r[layer],
            lru_w_i[layer], lru_b_i[layer], w_proj_a[layer], w_proj_b[layer], w_out[layer])
        h_lat = h_lat + mod_l[2] * mix_lat

        f_lat = modulate(rmsnorm(h_lat, g_norm2[layer]), mod_l[3], mod_l[4])
        h_lat = h_lat + mod_l[5] * peer_ffn(f_lat, peer_w_query[layer], peer_sub_keys[layer], peer_u[layer], peer_v[layer])

        if need_ctx:
            h_ctx = h_ctx + mod_c[2] * mix_ctx
            f_ctx = modulate(rmsnorm(h_ctx, g_norm2[layer]), mod_c[3], mod_c[4])
            h_ctx = h_ctx + mod_c[5] * peer_ffn(f_ctx, peer_w_query[layer], peer_sub_keys[layer], peer_u[layer], peer_v[layer])
    return rmsnorm(h_lat, g_final)


_drawn_inputs = setup_inputs


def setup_inputs(seed=0):
    import zlib

    import numpy as np

    out = dict(_drawn_inputs(seed))
    spreads = {}
    factors = {'b_ada': 3.473,
     'g_norm1': 7.246,
     's5_a_re': 64.0,
     's5_a_im': 58.64,
     's5_log_dt': 62.936,
     's5_b_re': 64.0,
     's5_b_im': 64.0,
     's5_c_re': 64.0,
     's5_c_im': 64.0,
     'lru_conv_b': 4.253,
     'lru_b_r': 50.435,
     'lru_b_i': 43.03,
     'g_norm2': 48.543,
     'g_final': 8.246}
    for name, (base, spread) in spreads.items():
        noise = np.random.default_rng([zlib.crc32(name.encode()), seed]).standard_normal(out[name].shape)
        drawn = base * np.exp(spread * noise) if base else spread * noise
        out[name] = jnp.asarray(drawn.astype(out[name].dtype))
    for name, factor in factors.items():
        out[name] = (out[name] * factor).astype(out[name].dtype)
    return out
```

```python
from contextlib import ExitStack

import numpy as np

import concourse.bass as bass
from concourse import mybir

F32 = mybir.dt.float32
U32 = mybir.dt.uint32
ALU = mybir.AluOpType
ACT = mybir.ActivationFunctionType
AX = mybir.AxisListType

P = 128
D = 2048
T = 256
KD = D // P
W = D // 2
KW = W // P
GRID_W = 64
ROWS = T // GRID_W
EPS = 1e-6
LRU_C = 8.0
CONV = 4
G, H, N, Q = 64, 16, 64, 8
NC = 2 * T // Q
NL = T // Q
GS = 4
NSTAGE = G // GS
NB = 2 * Q + 1
COLS = 256
UK = 8
RING = 5
NKEYS, HEADS, TOPK = 128, 8, 16
NU, NV, NDIAG = RING + 2, 9, 8
TWO_PI_1 = 6.28125
TWO_PI_2 = float(np.float32(round((2 * np.pi - TWO_PI_1) * 2 ** 21) / 2 ** 21))
TWO_PI_3 = float(2 * np.pi - TWO_PI_1 - TWO_PI_2)
PI = float(np.nextafter(np.float32(np.pi), np.float32(0)))
MAGIC = 1.5 * 2 ** 23
LOWEST = -3.0e38

def build(nc, t):
    ctx = ExitStack()
    with ctx:
        def sb(name, shape, dt=F32, stack=ctx):
            return stack.enter_context(nc.sbuf_tensor(name, shape, dt))[(slice(None),) * len(shape)]

        def sem(name):
            return ctx.enter_context(nc.semaphore(name))

        gates_dram = nc.dram_tensor("gates_dram", (2 * KD, P, T), F32, kind="Internal").ap()
        mods_dram = nc.dram_tensor("mods_dram", (2, 6 * D), F32, kind="Internal").ap()
        u_dram = nc.dram_tensor("u_dram", (KW, P, Q, NC), F32, kind="Internal").ap()
        y_dram = nc.dram_tensor("y_dram", (Q, H, G, NL), F32, kind="Internal").ap()

        w_ring = sb("w_ring", [P, RING, UK, COLS])
        ident = sb("ident", [P, P])
        mT = sb("mT", [P, KD, T])

        w_ada = t["w_ada"].rearrange("a (k p) n -> a p k n", p=P)[0]
        w_in = t["w_in"].rearrange("a (k p) n -> a p k n", p=P)[0]
        w_glu = t["s5_w_glu"].rearrange("a (k p) n -> a p k n", p=P)[0]
        w_pa = t["w_proj_a"].rearrange("a (k p) n -> a p k n", p=P)[0]
        w_pb = t["w_proj_b"].rearrange("a (k p) n -> a p k n", p=P)[0]
        w_out = t["w_out"].rearrange("a (k p) n -> a p k n", p=P)[0]
        w_q = t["peer_w_query"].rearrange("a (k p) n -> a p k n", p=P)[0]

        acc_full, acc_free = sem("acc_full"), sem("acc_free")
        unit_done, ada_used = sem("unit_done"), sem("ada_used")
        fin_full, fin_used = sem("fin_full"), sem("fin_used")
        out_full, out_used = sem("out_full"), sem("out_used")
        q_full, q_used = sem("q_full"), sem("q_used")
        w_in_sem = [sem(f"w_landed{i}") for i in range(RING)]

        units = []
        n_done = [0]

        def plan_pair(w, c, s, count):
            n_done[0] += 1
            units.append((w[:, 0:UK, c * COLS:(c + 1) * COLS], unit_done, n_done[0]))
            units.append((w[:, UK:KD, c * COLS:(c + 1) * COLS], s, count))

        acc = 0
        for c in range(16):
            acc += 1
            plan_pair(w_ada, c, acc_full, acc)
        for first in (W // COLS, 0):
            for c in range(W // COLS):
                acc += 2
                plan_pair(w_in, first + c, acc_full, acc)
        for c in range(W // COLS):
            acc += 2
            plan_pair(w_in, 2 * W // COLS + c, acc_full, acc)
        for s in range(NSTAGE):
            acc += 2
            plan_pair(w_in, 3 * W // COLS + s, acc_full, acc)
            acc += 1
            for x in range(4):
                w = w_ada[:, (x % 2) * UK:(x % 2 + 1) * UK]
                c = 16 + 2 * s + x // 2
                units.append((w[:, :, c * COLS:(c + 1) * COLS], ada_used, 4 * s + x + 1))
        for c in range(W // COLS):
            acc += 2
            units.append((w_glu[:, :, c * COLS:(c + 1) * COLS], acc_full, acc))
        NFIN = D // COLS
        for c in range(NFIN):
            units.append((w_pa[:, :, c * COLS:(c + 1) * COLS], fin_full, 2 * c + 1))
            units.append((w_pb[:, :, c * COLS:(c + 1) * COLS], fin_full, 2 * c + 2))
        for c in range(NFIN):
            plan_pair(w_out, c, out_full, c + 1)
        for c in range(NFIN):
            plan_pair(w_q, c, q_full, c + 1)

        def load_unit(eng, u):
            if u >= RING:
                eng.wait_ge(units[u - RING][1], units[u - RING][2])
            eng.dma_start(w_ring[:, u % RING], units[u][0]).then_inc(w_in_sem[u % RING], 16)

        def unit(pe, u):
            pe.wait_ge(w_in_sem[u % RING], 16 * (u // RING + 1))
            return w_ring[:, u % RING]

        mixer(nc, t, ctx, sem, w_ring, ident, mT, units, load_unit, unit, acc_full, acc_free, unit_done,
              ada_used, fin_full, fin_used, mods_dram, u_dram, y_dram, gates_dram)
        peer(nc, t, ctx, sem, w_ring, ident, mT, units, load_unit, unit, unit_done,
             out_full, out_used, q_full, q_used, mods_dram)


def stepper(eng, s):
    count = {}

    def link(ins, signal=None):
        x = s if signal is None else signal
        count[id(x)] = count.get(id(x), 0) + 1
        ins.then_inc(x, 1)
        eng.wait_ge(x, count[id(x)])
    return link


def mixer(nc, t, ctx, sem, w_ring, ident, mT, units, load_unit, unit, acc_full, acc_free, unit_done,
          ada_used, fin_full, fin_used, mods_dram, u_dram, y_dram, gates_dram):
    with ExitStack() as st:
        def sb(name, shape, dt=F32):
            return st.enter_context(nc.sbuf_tensor(name, shape, dt))[(slice(None),) * len(shape)]

        ps = st.enter_context(nc.psum_tensor("ps", [P, 8, 512], F32))[:, :, :]

        crow = sb("crow", [2 * KD, P])
        prow = sb("prow", [88, P])
        mrow = sb("mrow", [112, P])
        scol = sb("scol", [P, 2 * KD])
        pcol = sb("pcol", [P, 88])
        mcol = sb("mcol", [P, 112])
        nscale = sb("nscale", [P, 2, KD])
        nshift = sb("nshift", [P, 2, KD])
        modst = sb("modst", [2, 2, 2 * COLS])
        crow_sig = sb("crow_sig", [2 * KD, P])
        nT = sb("nT", [P, KD, 2 * T])
        xss = sb("xss", [P, 8])
        lsm = sb("lsm", [P, 8, 16])
        sp8 = sb("sp8", [P, 16])
        bd = mT[:, 0:KW, :].rearrange("p t (x c) -> p t x c", x=2)
        bd2 = mT[:, KW:KD, :].rearrange("p t (x c) -> p t x c", x=2)
        yl = mT[:, 0:KW, :]
        zu = sb("zu", [P, 2, Q, NC])
        U = nT[:, :, 0:T].rearrange("p k (g c) -> p k g c", g=GS)
        sqt = nT.rearrange("p k n -> p (k n)")[:, 0:D]
        ada_acc = zu.rearrange("p b s c -> p (b s c)").rearrange("p (j e n) -> p j e n", j=2, e=2)
        ones = sb("ones", [P, 1])
        gst = sb("gst", [P, 2, 2, T])
        sm = sb("sm", [P, 20, G])
        pP = sb("pP", [P, 2, G, Q])
        pwb = sb("pwb", [P, 2, G, NB])
        Cc = sb("Cc", [P, 2, G, H])
        Bb = sb("Bb", [P, 2, G, H])
        eb = sb("eb", [P, 2, G, 8])
        ea = sb("ea", [P, 2, G, 8])
        dT = sb("dT", [H, G])
        notfirst = sb("notfirst", [P, NC])
        big = sb("big", [P, 14656])

        xt = [big[:, i * D:(i + 1) * D] for i in range(4)]
        cnat = big[:, 4 * D:4 * D + 2 * KW * P].rearrange("p (r g n) -> p r g n", r=2, g=KW)
        anat = big[0:G, 4 * D + 2048:4 * D + 2048 + 256].rearrange("p (r n) -> p r n", r=2)
        dnat = big[0:G, 4 * D + 2304:4 * D + 2320]
        btmp = big[:, 4 * D + 2320:4 * D + 2320 + 2 * G * H].rearrange("p (r g h) -> p r g h", r=2, g=G)
        pw = big[:, 12560:12560 + 2 * 9 * G].rearrange("p (r g j) -> p r g j", r=2, g=G)
        o = [0]

        def take(n):
            o[0] += n
            return big[:, o[0] - n:o[0]]
        vraw = take(2 * 512).rearrange("p (b n) -> p b n", b=2)
        xc = take(4 * 512).rearrange("p (b n) -> p b n", b=4)
        rt = take(4 * 512).rearrange("p (b d n) -> p b d n", b=2, d=2)
        ig = take(4 * 512).rearrange("p (b d n) -> p b d n", b=2, d=2)
        ag = take(4 * 512).rearrange("p (b d n) -> p b d n", b=2, d=2)
        ltmp = take(2 * 512).rearrange("p (d n) -> p d n", d=2)
        o[0] = 0
        M = take(2 * 2 * GS * NB * H).rearrange("p (b r g n h) -> p b r g n h", b=2, r=2, g=GS, n=NB)
        Mt = take(GS * NB * H).rearrange("p (g n h) -> p g n h", g=GS, n=NB)
        PB = take(2 * GS * P).rearrange("p (r g s h) -> p r g s h", r=2, g=GS, s=Q)
        PBt = take(GS * P).rearrange("p (g s h) -> p g s h", g=GS, s=Q)
        PT = take(2 * 2 * GS * P).rearrange("p (b r g n) -> p b r g n", b=2, r=2, g=GS)
        kst = take(GS * (NB - 2) * H).rearrange("p (g n h) -> p g n h", g=GS, n=NB - 2)
        dg = take(GS * H).rearrange("p (g h) -> p g h", g=GS)
        Tz = take(2 * GS * P).rearrange("p (b g n) -> p b g n", b=2, g=GS)
        rot = take(3 * GS * NC).rearrange("p (x g c) -> p x g c", x=3, g=GS)
        Ssb = take(2 * GS * NC).rearrange("p (r g c) -> p r g c", r=2, g=GS)
        Sr = take(2 * GS * NC).rearrange("p (r g c) -> p r g c", r=2, g=GS)
        St = take(2 * GS * NC).rearrange("p (r g c) -> p r g c", r=2, g=GS)
        Rt = take(2 * GS * NC).rearrange("p (r g c) -> p r g c", r=2, g=GS)
        Hs = take(2 * 2 * GS * NL).rearrange("p (b r g c) -> p b r g c", b=2, r=2, g=GS)
        ysb = take(2 * GS * NL).rearrange("p (b g c) -> p b g c", b=2, g=GS)
        assert o[0] <= 14656, o
        o[0] = 0
        z5 = mT[:, KW:KD, :].rearrange("p k (s c) -> p k s c", s=Q)
        sg = take(2 * T).rearrange("p (b n) -> p b n", b=2)
        ya = take(KW * T).rearrange("p (k n) -> p k n", k=KW)
        yb = take(KW * T).rearrange("p (k n) -> p k n", k=KW)
        sgate = take(2 * 2 * 512).rearrange("p (b x n) -> p b x n", b=2, x=2)
        mt2 = take(2 * 512).rearrange("p (x n) -> p x n", x=2)

        id0, id_ready = sem("id0"), sem("id_ready")
        x_in = [sem(f"x_in{i}") for i in range(4)]
        rows_in, s5_in, b_in = sem("rows_in"), sem("s5_in"), sem("b_in")
        bd_zero, bd_in = sem("bd_zero"), sem("bd_in")
        silu_sig, silu_done, tr_setup, cols_done = sem("silu_sig"), sem("silu_done"), sem("tr_setup"), sem("cols_done")
        tr_s5, s5cols = sem("tr_s5"), sem("s5cols")
        ss_done, ms_done, rstd_done, xn_done = sem("ss_done"), sem("ms_done"), sem("rstd_done"), sem("xn_done")
        dt_done, re_done, tanh_done, th_done, sin_done = (sem("dt_done"), sem("re_done"), sem("tanh_done"),
                                                           sem("th_done"), sem("sin_done"))
        mrow_back = sem("mrow_back")
        fwd_done = sem("fwd_done")
        gst_out, sgate_in = [sem("gst_out0"), sem("gst_out1")], [sem("sgate_in0"), sem("sgate_in1")]
        ada_sum, gt_done = sem("ada_sum"), sem("gt_done")
        labs, lexp, sp_done = sem("labs"), sem("lexp"), sem("sp_done")
        mods_out, mrow_in, mcol_tr, norm_ready = sem("mods_out"), sem("mrow_in"), sem("mcol_tr"), sem("norm_ready")
        nt_tr, nt_ctx, nt_lat = sem("nt_tr"), sem("nt_ctx"), sem("nt_lat")
        conv_done, g_full, g_sig, et_done, q_ready, sq_done, lru_done = (
            sem("conv_done"), sem("g_full"), sem("g_sig"), sem("et_done"), sem("q_ready"), sem("sq_done"),
            sem("lru_done"))
        u_out, u_in, zu_free = sem("u_out"), sem("u_in"), sem("zu_free")
        m_done, pb_done, k_full, kst_done, x_full, pt_done = (sem("m_done"), sem("pb_done"), sem("k_full"),
                                                               sem("kst_done"), sem("x_full"), sem("pt_done"))
        t_in = [sem("t_in0"), sem("t_in1")]
        s_full, ssb_done, h_done, y_full, ysb_done = (sem("s_full"), sem("ssb_done"), sem("h_done"), sem("y_full"),
                                                       sem("ysb_done"))
        y_out, z5_in = [sem("y_out0"), sem("y_out1")], sem("z5_in")
        s5_setup, ssb_read = sem("s5_setup"), sem("ssb_read")
        gg_done, yb_done, sg_done, ya_done, sgate_done = (sem("gg_done"), sem("yb_done"), sem("sg_done"),
                                                          sem("ya_done"), sem("sgate_done"))
        dve, act_s, pool_s = sem("dve_step"), sem("act_step"), sem("pool_step")

        block = st.enter_context(nc.Block())
        A0, V0, U0, G0 = 0, 16, 24, 32
        S0 = G0 + KW
        L0 = S0 + 3 * NSTAGE
        STAGE_UNITS = 2 * (16 + 8 + 4)
        NUNITS_HERE = STAGE_UNITS + 6 * NSTAGE + 4 + 2 * (D // COLS)

        def toeplitz(sp, s):
            sp.wait_ge(kst_done, s + 1)
            if s >= 2:
                sp.wait_ge(y_full, s - 1)
            kv = kst.rearrange("p g n h -> p g (n h)")
            for i in range(Q):
                sp.dma_start(Tz[i * H:(i + 1) * H, s % 2], kv[0:H, :, (Q - 1 - i) * H:(2 * Q - 1 - i) * H])\
                  .then_inc(t_in[s % 2], 16)

        @block.sync
        def _(sp):
            crow_v = crow[:, :]
            sp.dma_start(crow_v[0:KD], t["c"].rearrange("a (k p) -> (a k) p", p=P)).then_inc(rows_in, 16)
            sp.dma_start(crow_v[KD:2 * KD], t["c_ctx"].rearrange("(k p) -> k p", p=P)).then_inc(rows_in, 16)
            sp.dma_start(prow[0:32], t["lru_conv_w"].rearrange("a w (k p) -> (a w k) p", p=P)).then_inc(rows_in, 16)
            sp.dma_start(prow[32:40], t["lru_conv_b"].rearrange("a (k p) -> (a k) p", p=P)).then_inc(rows_in, 16)
            sp.dma_start(prow[40:56], t["lru_lambda"].rearrange("a d (k p) -> (a d k) p", p=P)).then_inc(rows_in, 16)
            sp.dma_start(prow[56:72], t["lru_b_r"].rearrange("a d (k p) -> (a d k) p", p=P)).then_inc(rows_in, 16)
            sp.dma_start(prow[72:88], t["lru_b_i"].rearrange("a d (k p) -> (a d k) p", p=P)).then_inc(rows_in, 16)
            sp.dma_start(mrow[64:96], t["b_ada"][0, 0:2 * D].rearrange("(k p) -> k p", p=P)).then_inc(mrow_in, 16)
            sp.dma_start(mrow[96:112], t["g_norm1"].rearrange("a (k p) -> (a k) p", p=P)).then_inc(mrow_in, 16)
            for u in range(len(units)):
                if u == NUNITS_HERE + RING:
                    break
                s, x = divmod(u - STAGE_UNITS, 6)
                if x == 5 and 1 <= s <= NSTAGE:
                    toeplitz(sp, s - 1)
                load_unit(sp, u)

        @block.gpsimd
        def _(pool):
            link = stepper(pool, pool_s)
            pool.memset(ident[:], 0.0).then_inc(id0, 1)
            pool.wait_ge(id0, 1)
            pool.affine_select(out=ident[:], in_=ident[:], compare_op=ALU.not_equal, fill=1.0, base=0,
                               pattern=[[-1, P]], channel_multiplier=1).then_inc(id_ready, 1)
            for r, name in enumerate(("s5_a_re", "s5_a_im")):
                pool.dma_start(anat[:, r, :].rearrange("g (d n) -> g d n", d=2),
                               t[name].rearrange("a d g n -> g (a d) n")).then_inc(s5_in, 16)
            for d in range(2):
                src = t["s5_log_dt"][0, d:d + 1, :].to_broadcast([N, G])
                pool.dma_start(sm[d * N:(d + 1) * N, 0, :], src).then_inc(s5_in, 16)
            pool.dma_start(dnat, t["s5_d"].rearrange("a (g h) -> (a g) h", h=H)).then_inc(s5_in, 16)
            for r, name in enumerate(("s5_c_re", "s5_c_im")):
                for d in range(2):
                    pool.dma_start(cnat[:, r, :, d * N:(d + 1) * N],
                                   t[name][0, d].rearrange("(k g) h n -> (g h) k n", g=8)).then_inc(s5_in, 16)
            for r, name in enumerate(("s5_b_re", "s5_b_im")):
                for d in range(2):
                    pool.dma_start(Bb[d * N:(d + 1) * N, r], t[name][0, d].rearrange("g n h -> n g h"))\
                        .then_inc(b_in, 16)
            pool.memset(mT[:], 0.0).then_inc(bd_zero, 1)
            pool.wait_ge(bd_zero, 1)
            for d, dst in enumerate((bd, bd2)):
                for x, name in enumerate(("lru_w_r", "lru_w_i")):
                    src = t[name][0, d].rearrange("(k e) i j -> e i k j", e=2)
                    for e in range(2):
                        pool.dma_start(dst[e * 64:(e + 1) * 64, :, x, e * 64:(e + 1) * 64], src[e])\
                            .then_inc(bd_in, 16)

            def store_mods(q):
                rows = 2 if q < 8 else 1
                pool.wait_ge(acc_free, A0 + 2 * q + 2 if q < 8 else S0 + 3 * (q - 8) + 3)
                pool.dma_start(mods_dram[0:rows, q * 2 * COLS:(q + 1) * 2 * COLS], modst[0:rows, q % 2])\
                    .then_inc(mods_out, 16)
                pool.wait_ge(mods_out, 16 * (q + 1))

            for q in range(8):
                store_mods(q)
            for j, (row, m) in enumerate(((0, 0), (0, 1), (1, 0), (1, 1))):
                pool.dma_start(mrow[16 * j:16 * j + 16], mods_dram[row, m * D:(m + 1) * D]
                               .rearrange("(k p) -> k p", p=P)).then_inc(mrow_back, 16)
            for k in range(KW):
                pool.wait_ge(acc_free, U0 + k + 1)
                pool.dma_start(u_dram[k], zu[:, k % 2]).then_inc(u_out, 16)
                pool.wait_ge(u_out, 16 * (k + 1))
            for s in range(Q):
                for g in range(GS):
                    src = u_dram[:, :, s, :].rearrange("k (a b h) c -> b h (k a) c", h=H, b=GS)[g]
                    pool.dma_start(U[s * H:(s + 1) * H, :, g, :], src).then_inc(u_in, 16)

            def build_pb(s):
                g = slice(s * GS, (s + 1) * GS)
                pr, pi = (pP[:, r, g, :].unsqueeze(3).to_broadcast([P, GS, Q, H]) for r in range(2))
                br, bi = (Bb[:, r, g, :].unsqueeze(2).to_broadcast([P, GS, Q, H]) for r in range(2))
                if s >= 1:
                    pool.wait_ge(x_full, s)
                link(pool.tensor_tensor(PB[:, 0], pr, br, ALU.mult))
                link(pool.tensor_tensor(PBt, pi, bi, ALU.mult))
                link(pool.tensor_tensor(PB[:, 0], PB[:, 0], PBt, ALU.subtract))
                link(pool.tensor_tensor(PB[:, 1], pr, bi, ALU.mult))
                link(pool.tensor_tensor(PBt, pi, br, ALU.mult))
                pool.tensor_tensor(PB[:, 1], PB[:, 1], PBt, ALU.add).then_inc(pb_done, 1)
                pool.wait_ge(pb_done, s + 1)

            pool.wait_ge(s5_setup, 4)
            pool.wait_ge(lru_done, KW)
            build_pb(0)
            for s in range(NSTAGE + 2):
                if s >= 2:
                    pool.wait_ge(ysb_done, s - 1)
                    r = s - 2
                    pool.dma_start(y_dram[:, :, r * GS:(r + 1) * GS, :].rearrange("s h g c -> (s h) g c"),
                                   ysb[:, r % 2]).then_inc(y_out[r % 2], 16)
                    if r % 2 == 1:
                        for i in range(2):
                            pool.wait_ge(y_out[i], 16 * (r // 2 + 1))
                        for g in range(8):
                            pool.dma_start(z5[g * H:(g + 1) * H, r // 2],
                                           y_dram[:, :, (r // 2) * 8 + g, :].rearrange("s h c -> h s c"))\
                                .then_inc(z5_in, 16)
                if s < NSTAGE:
                    pool.wait_ge(acc_free, S0 + 3 * s + 2)
                    pool.dma_start(gates_dram[2 * s:2 * s + 2].rearrange("k p n -> p k n"), gst[:, s % 2])\
                        .then_inc(gst_out[s % 2], 16)
                    store_mods(8 + s)
                if s + 1 < NSTAGE:
                    build_pb(s + 1)
            for i in range(2):
                pool.wait_ge(gst_out[i], 16 * NSTAGE // 2)
            pool.wait_ge(acc_free, L0)
            for c in range(D // COLS):
                if c >= 2:
                    pool.wait_ge(fin_used, 3 * (c - 1))
                for x in range(2):
                    pool.dma_start(sgate[:, c % 2, x].rearrange("p (k n) -> p k n", k=2),
                                   gates_dram[x * KD + 2 * c:x * KD + 2 * c + 2].rearrange("k p n -> p k n"))\
                        .then_inc(sgate_in[c % 2], 16)

        @block.scalar
        def _(act):
            link = stepper(act, act_s)
            for i in range(4):
                src = (t["ctx"] if i < 2 else t["x"])[0, (i % 2) * P:(i % 2 + 1) * P, :]
                act.dma_start(xt[i], src).then_inc(x_in[i], 16)
            act.wait_ge(rows_in, 16 * 7)
            act.activation(crow_sig, crow[:, :], ACT.Sigmoid).then_inc(silu_sig, 1)
            for i in range(4):
                act.wait_ge(x_in[i], 16)
                act.activation(sqt, xt[i], ACT.Square, accum_out=xss[:, i:i + 1]).then_inc(ss_done, 1)
                act.wait_ge(ss_done, i + 1)
            act.wait_ge(s5_in, 16 * 9)
            act.activation(sm[:, 1, :], sm[:, 0, :], ACT.Exp).then_inc(dt_done, 1)
            act.wait_ge(labs, 1)
            act.activation(lsm[:, 1], lsm[:, 0], ACT.Exp, scale=-1.0).then_inc(lexp, 1)
            act.wait_ge(re_done, 1)
            act.activation(sm[:, 6, :], sm[:, 4, :], ACT.Tanh, scale=0.5).then_inc(tanh_done, 1)
            act.wait_ge(th_done, 1)
            act.activation(sm[:, 8, :], sm[:, 7, :], ACT.Sin).then_inc(sin_done, 1)
            act.activation(sm[:, 9, :], sm[:, 7, :], ACT.Sin, scale=0.5).then_inc(sin_done, 1)
            act.wait_ge(ms_done, 1)
            act.activation(xss[:, 4:8], xss[:, 4:8], ACT.Sqrt).then_inc(rstd_done, 1)
            act.wait_ge(rstd_done, 1)
            for i in range(4):
                act.activation(xt[i], xt[i], ACT.Copy, scale=xss[:, 4 + i:5 + i]).then_inc(xn_done, 1)

            def mod_rows(a, c):
                act.wait_ge(acc_full, a + 1)
                if c % 2 == 0 and c >= 4:
                    act.wait_ge(mods_out, 16 * (c // 2 - 1))
                act.activation(modst[:, (c // 2) % 2, (c % 2) * COLS:(c % 2 + 1) * COLS], ps[0:2, a % 2, 0:COLS],
                               ACT.Copy).then_inc(acc_free, 1)
            for c in range(16):
                mod_rows(A0 + c, c)
            act.wait_ge(norm_ready, 1)
            for k in range(KD):
                act.wait_ge(nt_tr, k + 1)
                act.activation(nT[:, k, 0:T], ps[:, 2 + k % 2, 0:T], ACT.Identity, scale=nscale[:, 1, k:k + 1],
                               bias=nshift[:, 1, k:k + 1]).then_inc(nt_ctx, 1)

            def gates(k):
                b = k % 2
                if k >= 2:
                    act.wait_ge(lru_done, k - 1)
                for n in range(4):
                    d, x = n // 2, n % 2
                    act.wait_ge(g_full, 4 * k + n + 1)
                    act.activation((rt, ig)[x][:, b, d, :], ps[:, 2 + n, :], ACT.Sigmoid,
                                   bias=pcol[:, 56 + 16 * x + 8 * d + k:57 + 16 * x + 8 * d + k]).then_inc(g_sig, 1)
                act.wait_ge(g_sig, 4 * k + 4)
                for d in range(2):
                    act.activation(ag[:, b, d, :], rt[:, b, d, :], ACT.Exp, scale=lsm[:, 7, 8 * d + k:8 * d + k + 1])\
                        .then_inc(et_done, 1)
                for d in range(2):
                    act.wait_ge(et_done, 4 * k + d + 1)
                    act.activation(rt[:, b, d, :], rt[:, b, d, :], ACT.Tanh, scale=sp8[:, 8 * d + k:8 * d + k + 1])\
                        .then_inc(et_done, 1)

            def roots(k):
                act.wait_ge(q_ready, k + 1)
                for d in range(2):
                    act.activation(rt[:, k % 2, d, :], rt[:, k % 2, d, :], ACT.Sqrt).then_inc(sq_done, 1)

            for i in range(2 * KW):
                act.wait_ge(acc_full, V0 + i + 1)
                if i < KW:
                    if i == 0:
                        act.wait_ge(nt_tr, KD)
                    if i >= 2:
                        act.wait_ge(conv_done, i - 1)
                    link(act.activation(vraw[:, i % 2, 0:T], ps[:, i % 2, 0:T], ACT.Copy))
                    act.activation(vraw[:, i % 2, T:2 * T].rearrange("p (w r) -> p w r", r=ROWS),
                                   ps[:, i % 2, T:2 * T].rearrange("p (r w) -> p w r", w=GRID_W), ACT.Copy)\
                        .then_inc(acc_free, 1)
                else:
                    k = i - KW
                    if k >= 2:
                        act.wait_ge(u_out, 16 * (k - 1))
                    act.activation(zu[:, k % 2], ps[:, i % 2, :].rearrange("p (c s) -> p s c", s=Q), ACT.Copy)\
                        .then_inc(acc_free, 1)
                if 1 <= i <= KW:
                    gates(i - 1)
                if 2 <= i <= KW + 1:
                    roots(i - 2)

            def evac_pt(s):
                act.wait_ge(x_full, s + 1)
                if s >= 2:
                    act.wait_ge(s_full, s - 1)
                act.activation(PT[:, s % 2].rearrange("p r g n -> p r (g n)"), ps[:, 4:6, :], ACT.Copy)\
                    .then_inc(pt_done, 1)

            def evac_s(s):
                act.wait_ge(s_full, s + 1)
                if s >= 1:
                    act.wait_ge(ssb_read, s)
                v = ps[:, 6, :].rearrange("p (x c) -> p x c", c=NC)
                o_ = Ssb.rearrange("p r g c -> p (r g) c")
                act.activation(o_[0:N], v[0:N], ACT.Copy).then_inc(ssb_done, 1)
                for h_ in range(2):
                    c = slice(h_ * NL, (h_ + 1) * NL)
                    act.activation(o_[N:P, :, c], v[N:P, :, c][:, :, ::-1], ACT.Copy).then_inc(ssb_done, 1)

            def evac_y(s):
                act.wait_ge(y_full, s + 1)
                if s >= 2:
                    act.wait_ge(y_out[s % 2], 16 * (s // 2))
                act.activation(ysb[:, s % 2].rearrange("p g c -> p (g c)"), ps[:, 7, 0:GS * NL], ACT.Gelu_apprx_tanh)\
                    .then_inc(ysb_done, 1)

            for k in range(KW):
                act.wait_ge(acc_full, G0 + k + 1)
                if k >= 2:
                    act.wait_ge(yb_done, k - 1)
                act.activation(gst[:, k % 2, 0], ps[:, k % 2, 0:T], ACT.Gelu_apprx_tanh).then_inc(acc_free, 1)

            def gate(s, j):
                a = S0 + 3 * s + j
                act.wait_ge(acc_full, a + 1)
                if s == 0:
                    act.wait_ge(yb_done, KW)
                if s >= 2:
                    act.wait_ge(gst_out[s % 2], 16 * (s // 2))
                act.activation(gst[:, s % 2, j], ps[:, a % 2, 0:T], ACT.Sigmoid).then_inc(acc_free, 1)

            def mod_sums(s):
                a = S0 + 3 * s + 2
                act.wait_ge(acc_full, a + 1)
                act.wait_ge(mods_out, 16 * (8 + s - 1))
                act.activation(modst[0:1, s % 2], ps[0:1, a % 2, :], ACT.Copy).then_inc(acc_free, 1)

            for s in range(NSTAGE + 2):
                if s < NSTAGE:
                    gate(s, 0)
                    gate(s, 1)
                if s >= 2:
                    evac_y(s - 2)
                if s < NSTAGE:
                    evac_pt(s)
                if 1 <= s <= NSTAGE:
                    evac_s(s - 1)
                if s < NSTAGE:
                    mod_sums(s)
            act.wait_ge(h_done, NSTAGE * 4)
            for k in range(KW):
                act.wait_ge(acc_full, L0 + k + 1)
                if k >= 2:
                    act.wait_ge(ya_done, k - 1)
                act.activation(sg[:, k % 2], ps[:, k % 2, 0:T], ACT.Sigmoid).then_inc(acc_free, 1)

        @block.vector
        def _(v):
            link = stepper(v, dve)
            v.memset(notfirst[:], 1.0).then_inc(dve, 1)
            link_base = [1]
            v.wait_ge(dve, 1)

            def step(ins):
                link_base[0] += 1
                ins.then_inc(dve, 1)
                v.wait_ge(dve, link_base[0])
            tt, tsc, stt = v.tensor_tensor, v.tensor_scalar, v.scalar_tensor_tensor
            step(v.memset(notfirst[:, 0:1], 0.0))
            step(v.memset(ones[:], 1.0))
            v.wait_ge(silu_sig, 1)
            tt(crow[:], crow[:], crow_sig, ALU.mult).then_inc(silu_done, 1)
            v.wait_ge(tr_setup, 2)
            v.tensor_copy(scol[:], ps[:, 2, 0:32]).then_inc(cols_done, 1)
            step(v.tensor_copy(pcol[:], ps[:, 2, 32:120]))
            lam = pcol[:, 40:56]
            step(tsc(lsm[:, 2], lam, -1.0, None, ALU.mult))
            tt(lsm[:, 0], lam, lsm[:, 2], ALU.max).then_inc(labs, 1)
            v.wait_ge(lexp, 1)
            step(tsc(lsm[:, 3], lsm[:, 1], 2.0, None, ALU.add))
            step(v.reciprocal(lsm[:, 3], lsm[:, 3]))
            step(tt(lsm[:, 3], lsm[:, 3], lsm[:, 1], ALU.mult))
            step(tt(lsm[:, 4], lsm[:, 3], lsm[:, 3], ALU.mult))
            step(tsc(lsm[:, 5], lsm[:, 4], 1.0 / 17, 1.0 / 15, ALU.mult, ALU.add))
            for n in (13, 11, 9, 7, 5, 3, 1):
                step(tt(lsm[:, 5], lsm[:, 5], lsm[:, 4], ALU.mult))
                step(tsc(lsm[:, 5], lsm[:, 5], 1.0 / n, None, ALU.add))
            step(tt(lsm[:, 5], lsm[:, 5], lsm[:, 3], ALU.mult))
            step(tsc(lsm[:, 5], lsm[:, 5], 2.0 * LRU_C, None, ALU.mult))
            step(tsc(lsm[:, 2], lsm[:, 2], 0.0, LRU_C, ALU.max, ALU.mult))
            step(tt(sp8[:], lsm[:, 5], lsm[:, 2], ALU.add))
            tsc(lsm[:, 7], sp8[:], -1.0, None, ALU.mult).then_inc(sp_done, 1)
            v.wait_ge(sp_done, 1)
            v.wait_ge(ss_done, 4)
            step(tsc(xss[:, 4:8], xss[:, 0:4], 1.0 / D, EPS, ALU.mult, ALU.add))
            v.reciprocal(xss[:, 4:8], xss[:, 4:8]).then_inc(ms_done, 1)
            DT, AR, AI, RE, IM, TH, RED, SN, SH = 1, 2, 3, 4, 5, 6, 7, 8, 9
            s_ = lambda i: sm[:, i, :]
            v.wait_ge(tr_s5, 1)
            step(v.tensor_copy(sm[:, AR:AI + 1, :].rearrange("p x g -> p (x g)"), ps[:, 3, 0:2 * G]))
            step(v.tensor_copy(dT[:], ps[0:H, 3, 2 * G:3 * G]))
            v.wait_ge(dt_done, 1)
            step(tt(s_(IM), s_(AI), s_(DT), ALU.mult))
            tt(s_(RE), s_(AR), s_(DT), ALU.mult).then_inc(re_done, 1)
            step(tsc(s_(10), s_(IM), 1.0 / (2 * np.pi), MAGIC, ALU.mult, ALU.add))
            step(tsc(s_(10), s_(10), MAGIC, None, ALU.subtract))
            step(stt(s_(RED), s_(10), -TWO_PI_1, s_(IM), ALU.mult, ALU.add))
            step(stt(s_(RED), s_(10), -TWO_PI_2, s_(RED), ALU.mult, ALU.add))
            step(stt(s_(RED), s_(10), -TWO_PI_3, s_(RED), ALU.mult, ALU.add))
            tsc(s_(RED), s_(RED), PI, -PI, ALU.min, ALU.max).then_inc(th_done, 1)
            v.wait_ge(tanh_done, 1)
            EM, R1, CM, CS, XR, XI, CR, CI, DEN = 10, 11, 12, 13, 14, 15, 16, 17, 18
            step(tsc(s_(R1), s_(TH), -1.0, 1.0, ALU.mult, ALU.add))
            step(v.reciprocal(s_(R1), s_(R1)))
            step(stt(s_(EM), s_(TH), 2.0, s_(R1), ALU.mult, ALU.mult))
            step(tsc(s_(R1), s_(EM), 1.0, None, ALU.add))
            v.wait_ge(sin_done, 2)
            step(stt(s_(CM), s_(SH), -2.0, s_(SH), ALU.mult, ALU.mult))
            step(tsc(s_(CS), s_(CM), 1.0, None, ALU.add))
            step(tt(s_(XR), s_(EM), s_(CS), ALU.mult))
            step(tt(s_(XR), s_(XR), s_(CM), ALU.add))
            step(tt(s_(XI), s_(R1), s_(SN), ALU.mult))
            step(tt(s_(DEN), s_(AR), s_(AR), ALU.mult))
            step(tt(s_(CR), s_(AI), s_(AI), ALU.mult))
            step(tt(s_(DEN), s_(DEN), s_(CR), ALU.add))
            step(v.reciprocal(s_(DEN), s_(DEN)))
            step(tt(s_(CR), s_(XR), s_(AR), ALU.mult))
            step(tt(s_(CI), s_(XI), s_(AI), ALU.mult))
            step(tt(s_(CR), s_(CR), s_(CI), ALU.add))
            step(tt(s_(CR), s_(CR), s_(DEN), ALU.mult))
            step(tt(s_(CI), s_(XI), s_(AR), ALU.mult))
            step(tt(s_(6), s_(XR), s_(AI), ALU.mult))
            step(tt(s_(CI), s_(CI), s_(6), ALU.subtract))
            step(tt(s_(CI), s_(CI), s_(DEN), ALU.mult))

            def cmul(o_re, o_im, ar, ai, br, bi, t1, t2):
                step(tt(t1, ai, bi, ALU.mult))
                step(tt(t2, ar, bi, ALU.mult))
                step(tt(o_re, ar, br, ALU.mult))
                step(tt(o_im, ai, br, ALU.mult))
                step(tt(o_re, o_re, t1, ALU.subtract))
                step(tt(o_im, o_im, t2, ALU.add))

            v.wait_ge(b_in, 16 * 4)
            cr, ci = (s_(x).unsqueeze(2).to_broadcast([P, G, H]) for x in (CR, CI))
            step(tt(btmp[:, 0], ci, Bb[:, 1], ALU.mult))
            step(tt(btmp[:, 1], ci, Bb[:, 0], ALU.mult))
            step(tt(Bb[:, 0], cr, Bb[:, 0], ALU.mult))
            step(tt(Bb[:, 1], cr, Bb[:, 1], ALU.mult))
            step(tt(Bb[:, 0], Bb[:, 0], btmp[:, 0], ALU.subtract))
            step(tt(Bb[:, 1], Bb[:, 1], btmp[:, 1], ALU.add))

            def chain(dst, n, base_re, base_im):
                step(v.memset(dst[:, 0, :, 0:1], 1.0))
                step(v.memset(dst[:, 1, :, 0:1], 0.0))
                step(v.tensor_copy(dst[:, 0, :, 1], base_re))
                step(v.tensor_copy(dst[:, 1, :, 1], base_im))
                for j in range(2, n):
                    cmul(dst[:, 0, :, j], dst[:, 1, :, j], dst[:, 0, :, j - 1], dst[:, 1, :, j - 1], base_re, base_im,
                         s_(6), s_(7))
            step(tsc(s_(XR), s_(XR), 1.0, None, ALU.add))
            chain(pw, 9, s_(XR), s_(XI))
            er, ei = s_(CS), s_(SN)
            nr, ni = s_(8 + 6), s_(8 + 7)
            for i in range(3):
                step(tt(s_(R1), s_(R1), s_(R1), ALU.mult))

            def square(o_re, o_im, a_re, a_im):
                step(tt(s_(6), a_re, a_re, ALU.mult))
                step(tt(s_(7), a_im, a_im, ALU.mult))
                step(stt(o_im, a_re, 2.0, a_im, ALU.mult, ALU.mult))
                step(tt(o_re, s_(6), s_(7), ALU.subtract))
            for i in range(3):
                square(nr, ni, er, ei)
                er, ei, nr, ni = nr, ni, er, ei
            chain(eb, 8, er, ei)
            for i in range(3):
                square(nr, ni, er, ei)
                er, ei, nr, ni = nr, ni, er, ei
            chain(ea, 8, er, ei)
            step(v.memset(pwb[:], 0.0))
            for r in range(2):
                step(v.tensor_copy(pwb[0:N, r, :, Q:NB], pw[0:N, r, :, 0:Q + 1]))
                step(v.tensor_copy(pwb[N:P, r, :, 0:Q + 1], pw[N:P, r, :, ::-1]))
                step(v.tensor_copy(pP[0:N, r], pw[0:N, r, :, 0:Q][:, :, ::-1]))
                step(v.tensor_copy(pP[N:P, r], pw[N:P, r, :, 0:Q]))
            v.wait_ge(tr_s5, 2)
            for b in range(4):
                v.tensor_copy(Cc[:, b // 2, (b % 2) * 32:(b % 2) * 32 + 32, :].rearrange("p g h -> p (g h)"),
                              ps[:, 4 + b, :]).then_inc(s5_setup, 1)
            v.wait_ge(s5_setup, 4)

            v.wait_ge(mcol_tr, 1)
            step(v.tensor_copy(mcol[:], ps[:, 2, 0:112]))
            for x in range(2):
                step(tt(nshift[:, x], mcol[:, 32 * x:32 * x + 16], mcol[:, 64:80], ALU.add))
                step(tt(nscale[:, x], mcol[:, 32 * x + 16:32 * x + 32], mcol[:, 80:96], ALU.add))
                step(tsc(nscale[:, x], nscale[:, x], 1.0, None, ALU.add))
                if x == 0:
                    step(tt(nscale[:, x], nscale[:, x], mcol[:, 96:112], ALU.mult))
                else:
                    tt(nscale[:, x], nscale[:, x], mcol[:, 96:112], ALU.mult).then_inc(norm_ready, 1)
            for k in range(KD):
                v.wait_ge(nt_tr, k + 1)
                tsc(nT[:, k, T:2 * T], ps[:, 4 + k % 2, 0:T], nscale[:, 0, k:k + 1], nshift[:, 0, k:k + 1],
                    ALU.mult, ALU.add).then_inc(nt_lat, 1)

            def conv(k):
                v.wait_ge(acc_free, V0 + k + 1)
                if k >= 4:
                    v.wait_ge(g_full, 4 * (k - 3))
                src, dst = vraw[:, k % 2], xc[:, k % 4]
                cw = [pcol[:, 8 * j + k:8 * j + k + 1] for j in range(CONV)]
                step(tsc(dst, src, cw[1], pcol[:, 32 + k:33 + k], ALU.mult, ALU.add))
                sl, dl = (a[:, T:2 * T].rearrange("p (w r) -> p w r", r=ROWS) for a in (src, dst))
                for j in (0, 2, 3):
                    lo, hi = max(0, 1 - j), max(0, j - 1)
                    step(stt(dst[:, lo:T - hi], src[:, lo + j - 1:T - hi + j - 1], cw[j], dst[:, lo:T - hi],
                             ALU.mult, ALU.add))
                    ins = stt(dl[:, :, lo:ROWS - hi], sl[:, :, lo + j - 1:ROWS - hi + j - 1], cw[j],
                              dl[:, :, lo:ROWS - hi], ALU.mult, ALU.add)
                    if j < 3:
                        step(ins)
                    else:
                        ins.then_inc(conv_done, 1)
                        v.wait_ge(conv_done, k + 1)

            def q_of(k):
                v.wait_ge(et_done, 4 * k + 4)
                b = k % 2
                step(tsc(ltmp, rt[:, b], 1.0, None, ALU.add))
                step(v.reciprocal(ltmp, ltmp))
                stt(rt[:, b], rt[:, b], 2.0, ltmp, ALU.mult, ALU.mult).then_inc(q_ready, 1)
                v.wait_ge(q_ready, k + 1)

            def scans(k):
                b = k % 2
                v.wait_ge(sq_done, 2 * k + 2)
                for d in range(2):
                    step(tt(ig[:, b, d], ig[:, b, d], xc[:, k % 4], ALU.mult))
                    step(tt(ig[:, b, d], ig[:, b, d], rt[:, b, d], ALU.mult))
                fw = (ag[:, b, 0], ig[:, b, 0], rt[:, b, 0])
                step(v.tensor_tensor_scan(fw[2], fw[0], fw[1], 0.0, ALU.mult, ALU.add))
                for lo, first in ((0, 0.0), (T, rt[:, b, 1, 0:1])):
                    a_, b_, h_ = (x[:, b, 1, lo:lo + T][:, ::-1] for x in (ag, ig, rt))
                    step(v.tensor_tensor_scan(h_, a_, b_, first, ALU.mult, ALU.add))
                tt(yl[:, k], rt[:, b, 0, T:2 * T], rt[:, b, 1, T:2 * T], ALU.add).then_inc(lru_done, 1)
                v.wait_ge(lru_done, k + 1)

            for i in range(KW + 3):
                if i < KW:
                    conv(i)
                if 2 <= i <= KW + 1:
                    q_of(i - 2)
                if i >= 3:
                    scans(i - 3)

            def build_m(s):
                b, g = s % 2, slice(s * GS, (s + 1) * GS)
                pr, pi = (pwb[:, r, g, :].unsqueeze(3).to_broadcast([P, GS, NB, H]) for r in range(2))
                c_r, c_i = (Cc[:, r, g, :].unsqueeze(2).to_broadcast([P, GS, NB, H]) for r in range(2))
                if s >= 2:
                    v.wait_ge(y_full, s - 1)
                step(tt(M[:, b, 0], pr, c_r, ALU.mult))
                step(tt(Mt, pi, c_i, ALU.mult))
                step(tt(M[:, b, 0], M[:, b, 0], Mt, ALU.subtract))
                step(tt(M[:, b, 1], pr, c_i, ALU.mult))
                step(tt(Mt, pi, c_r, ALU.mult))
                fl = lambda a: a.rearrange("p g n h -> p (g n h)")
                stt(fl(M[:, b, 1]), fl(M[:, b, 1]), -1.0, fl(Mt), ALU.mult, ALU.subtract).then_inc(m_done, 1)
                v.wait_ge(m_done, s + 1)

            def evac_k(s):
                v.wait_ge(k_full, s + 1)
                if s >= 1:
                    v.wait_ge(t_in[(s - 1) % 2], 16 * Q * ((s - 1) // 2 + 1))
                g = slice(s * GS, (s + 1) * GS)
                step(tt(dg[0:H], ident[0:H, 0:H].unsqueeze(1).to_broadcast([H, GS, H]),
                        dT[:, g].unsqueeze(2).to_broadcast([H, GS, H]), ALU.mult))
                for x in range(2):
                    step(v.tensor_copy(kst[0:H, 2 * x:2 * x + 2].rearrange("p g n h -> p g (n h)"),
                                       ps[0:H, 2 + x, :].rearrange("p (g n) -> p g n", g=2)[:, :, 0:(NB - 2) * H]))
                tt(kst[0:H, :, Q - 1, :], kst[0:H, :, Q - 1, :], dg[0:H], ALU.add).then_inc(kst_done, 1)
                v.wait_ge(kst_done, s + 1)

            def rotations(s):
                g = slice(s * GS, (s + 1) * GS)
                sh = [P, GS, 8, 8]
                A_ = [ea[:, r, g, :].unsqueeze(3).to_broadcast(sh) for r in range(2)]
                B_ = [eb[:, r, g, :].unsqueeze(2).to_broadcast(sh) for r in range(2)]
                w = [rot[:, x].rearrange("p g (a b) -> p g a b", b=8) for x in range(3)]
                step(tt(w[0], A_[0], B_[0], ALU.mult))
                step(tt(w[2], A_[1], B_[1], ALU.mult))
                step(tt(w[0], w[0], w[2], ALU.subtract))
                step(tt(w[1], A_[0], B_[1], ALU.mult))
                step(tt(w[2], A_[1], B_[0], ALU.mult))
                step(tt(w[1], w[1], w[2], ALU.add))
                for r in range(2):
                    step(tt(Rt[:, r], notfirst[:].unsqueeze(1).to_broadcast([P, GS, NC]),
                            sm[:, 11, g].unsqueeze(2).to_broadcast([P, GS, NC]), ALU.mult))

            def state_scan(s):
                v.wait_ge(ssb_done, 3 * s + 3)
                for r, x in ((0, Sr), (1, St)):
                    ins = tt(x, Ssb, rot[:, r:r + 1].to_broadcast([P, 2, GS, NC]), ALU.mult)
                    if r == 0:
                        step(ins)
                    else:
                        ins.then_inc(ssb_read, 1)
                        v.wait_ge(ssb_read, s + 1)
                step(tt(Sr[:, 0], Sr[:, 0], St[:, 1], ALU.add))
                step(tt(Sr[:, 1], Sr[:, 1], St[:, 0], ALU.subtract))
                fl = lambda a: a.rearrange("p r g c -> p (r g c)")
                step(v.tensor_tensor_scan(fl(St), fl(Rt), fl(Sr), 0.0, ALU.mult, ALU.add))
                c = slice(NL - 1, 2 * NL - 1)
                gc = Sr[:, :, :, 0:NL]
                gs = Sr[:, :, :, NL:2 * NL]
                step(tt(gc, St[:, :, :, c], rot[:, 0:1, :, c].to_broadcast([P, 2, GS, NL]), ALU.mult))
                step(tt(gs, St[:, :, :, c], rot[:, 1:2, :, c].to_broadcast([P, 2, GS, NL]), ALU.mult))
                if s >= 2:
                    v.wait_ge(y_full, s - 1)
                for lo, hi, d in ((0, N, 1), (N, P, -1)):
                    h_ = Hs[lo:hi, s % 2]
                    tt(h_[:, 0, :, ::d], gc[lo:hi, 0], gs[lo:hi, 1], ALU.subtract).then_inc(h_done, 1)
                    tt(h_[:, 1, :, ::d], gc[lo:hi, 1], gs[lo:hi, 0], ALU.add).then_inc(h_done, 1)
                v.wait_ge(h_done, 4 * s + 4)

            def modulations(s):
                if s == 0:
                    v.wait_ge(u_out, 16 * KW)
                else:
                    v.wait_ge(acc_full, S0 + 3 * s)
                for x in range(4):
                    u = STAGE_UNITS + 6 * s + 2 + x
                    w = unit(v, u)
                    for k in range(UK):
                        kk = (x % 2) * UK + k
                        acc_ = ada_acc[:, x // 2, k % 2]
                        ins = (tsc(acc_, w[:, k, :], scol[:, kk:kk + 1], None, ALU.mult) if kk < 2 else
                               stt(acc_, w[:, k, :], scol[:, kk:kk + 1], acc_, ALU.mult, ALU.add))
                        if k == UK - 1:
                            ins.then_inc(ada_used, 1)
                            v.wait_ge(ada_used, 4 * s + x + 1)
                        else:
                            link_base[0] += 1
                            ins.then_inc(dve, 1)
                            v.wait_ge(dve, link_base[0] - (1 if k else 0))

            for k in range(KW):
                v.wait_ge(acc_free, G0 + k + 1)
                gk = gst[:, k % 2, 0]
                tt(gk.rearrange("p (r w) -> p r w", w=GRID_W), yl[:, k].rearrange("p (w r) -> p r w", r=ROWS),
                   gk.rearrange("p (r w) -> p r w", w=GRID_W), ALU.mult).then_inc(gt_done, 1)
                v.wait_ge(gt_done, k + 1)
                v.tensor_copy(yl[:, k], gk).then_inc(yb_done, 1)
                v.wait_ge(yb_done, k + 1)

            for s in range(NSTAGE + 2):
                if 1 <= s <= NSTAGE:
                    evac_k(s - 1)
                if s >= 2:
                    rotations(s - 2)
                    state_scan(s - 2)
                if s < NSTAGE:
                    build_m(s)
                    modulations(s)
            v.wait_ge(acc_full, L0 + 1)
            v.tensor_copy(yb.rearrange("p k n -> p (k n)"), yl.rearrange("p k n -> p (k n)")).then_inc(yb_done, 1)
            for k in range(KW):
                v.wait_ge(acc_free, L0 + k + 1)
                tt(ya[:, k].rearrange("p (c s) -> p s c", s=Q), z5[:, k],
                   sg[:, k % 2].rearrange("p (s c) -> p s c", s=Q), ALU.mult).then_inc(ya_done, 1)
            for c in range(D // COLS):
                v.wait_ge(sgate_in[c % 2], 32 * (c // 2 + 1))
                for x in range(2):
                    v.wait_ge(fin_full, 2 * c + x + 1)
                    tt(mt2[:, x], sgate[:, c % 2, x], ps[:, 2 + 2 * (c % 3) + x, :], ALU.mult).then_inc(fin_used, 1)
                v.wait_ge(fin_used, 3 * c + 2)
                tt(mT[:, 2 * c:2 * c + 2, :].rearrange("p k n -> p (k n)"), mt2[:, 0], mt2[:, 1], ALU.add)\
                    .then_inc(fin_used, 1)
                v.wait_ge(fin_used, 3 * c + 3)

        @block.tensor
        def _(pe):
            pe.wait_ge(id_ready, 1)
            pe.wait_ge(silu_done, 1)
            pe.transpose(ps[:, 2, 0:32], crow[:], ident[0:32, 0:32]).then_inc(tr_setup, 1)
            pe.transpose(ps[:, 2, 32:120], prow[:], ident[0:88, 0:88]).then_inc(tr_setup, 1)
            pe.wait_ge(s5_in, 16 * 9)
            for r in range(2):
                pe.transpose(ps[:, 3, r * G:(r + 1) * G], anat[:, r], ident[0:G, 0:G])
            pe.transpose(ps[0:H, 3, 2 * G:3 * G], dnat, ident[0:G, 0:G]).then_inc(tr_s5, 1)
            for r in range(2):
                for k in range(KW):
                    last = pe.transpose(ps[:, 4 + 2 * r + k // 4, (k % 4) * P:(k % 4 + 1) * P], cnat[:, r, k], ident[:])
            last.then_inc(tr_s5, 1)
            pe.wait_ge(cols_done, 1)
            sc = scol[:].rearrange("p (j k) -> p k j", j=2)
            n = [0]

            def free(a):
                if a >= 2:
                    pe.wait_ge(acc_free, a - 1)

            def mods(a):
                free(a)
                for h_ in range(2):
                    w = unit(pe, n[0])
                    n[0] += 1
                    for k in range(UK):
                        last = pe.matmul(ps[0:2, a % 2, 0:COLS], sc[:, h_ * UK + k, :], w[:, k, :],
                                         start=(h_ + k == 0), stop=(h_ * UK + k == KD - 1))
                    last.then_inc(unit_done if h_ == 0 else acc_full, 1)

            def columns(a, lo, hi):
                w = [unit(pe, n[0]), unit(pe, n[0] + 1)]
                n[0] += 2
                for j in range(2):
                    free(a + j)
                    for k in range(KD):
                        last = pe.matmul(ps[:, (a + j) % 2, 0:hi - lo], w[k // UK][:, k % UK, j * P:(j + 1) * P],
                                         nT[:, k, lo:hi], start=(k == 0), stop=(k == KD - 1))
                        if j == 1 and k == UK - 1:
                            last.then_inc(unit_done, 1)
                    last.then_inc(acc_full, 1)
                    yield

            for c in range(16):
                mods(A0 + c)
            pe.wait_ge(mrow_in, 16 * 2)
            pe.wait_ge(mrow_back, 16 * 4)
            pe.wait_ge(s5_setup, 4)
            pe.transpose(ps[:, 2, 0:112], mrow[:], ident[0:112, 0:112]).then_inc(mcol_tr, 1)
            pe.wait_ge(xn_done, 4)
            pe.wait_ge(norm_ready, 1)
            for k in range(KD):
                if k >= 2:
                    pe.wait_ge(nt_ctx, k - 1)
                    pe.wait_ge(nt_lat, k - 1)
                for i in range(4):
                    last = pe.transpose(ps[:, 2 + 2 * (i // 2) + k % 2, (i % 2) * P:(i % 2 + 1) * P], xt[i][:, k * P:(k + 1) * P], ident[:])
                last.then_inc(nt_tr, 1)
            pe.wait_ge(nt_ctx, KD)
            pe.wait_ge(nt_lat, KD)
            pe.wait_ge(bd_in, 16 * 8)

            def gates(k):
                pe.wait_ge(conv_done, k + 1)
                if k >= 1:
                    pe.wait_ge(g_sig, 4 * k)
                for i in range(4):
                    pe.matmul(ps[:, 2 + i, :], (bd, bd2)[i // 2][:, k, i % 2, :], xc[:, k % 4], start=True, stop=True)\
                        .then_inc(g_full, 1)

            i = 0
            for c in range(2 * KW // 2):
                for _ in columns(V0 + 2 * c, 0, 2 * T):
                    if 1 <= i <= KW:
                        gates(i - 1)
                    i += 1

            for c in range(KW // 2):
                for _ in columns(G0 + 2 * c, T, 2 * T):
                    pass

            def s5_params(s):
                b = s % 2
                pe.wait_ge(m_done, s + 1)
                if s >= 1:
                    pe.wait_ge(kst_done, s)
                else:
                    pe.wait_ge(g_sig, 4 * KW)
                for g in range(GS):
                    for r in range(2):
                        last = pe.matmul(ps[0:H, 2 + g // 2, (g % 2) * 256:(g % 2) * 256 + (NB - 2) * H],
                                         Bb[:, r, s * GS + g, :],
                                         M[:, b, r, g, 1:NB - 1, :].rearrange("p n h -> p (n h)"),
                                         start=(r == 0), stop=(r == 1))
                last.then_inc(k_full, 1)
                pe.wait_ge(pb_done, s + 1)
                if s >= 1:
                    pe.wait_ge(pt_done, s)
                for r in range(2):
                    for g in range(GS):
                        last = pe.transpose(ps[:, 4 + r, g * P:(g + 1) * P], PB[:, r, g].rearrange("p s h -> p (s h)"),
                                            ident[:])
                last.then_inc(x_full, 1)

            def s5_states(s):
                pe.wait_ge(pt_done, s + 1)
                pe.wait_ge(u_in, 16 * Q * GS)
                if s >= 1:
                    pe.wait_ge(ssb_done, 3 * s)
                for r in range(2):
                    for g in range(GS):
                        last = pe.matmul(ps[:, 6, (r * GS + g) * NC:(r * GS + g + 1) * NC], PT[:, s % 2, r, g, :],
                                         U[:, s, g, :], start=True, stop=True)
                last.then_inc(s_full, 1)

            def s5_out(s):
                b = s % 2
                pe.wait_ge(t_in[b], 16 * Q * (s // 2 + 1))
                pe.wait_ge(h_done, 4 * s + 4)
                if s >= 1:
                    pe.wait_ge(ysb_done, s)
                out = [ps[:, 7, g * NL:(g + 1) * NL] for g in range(GS)]
                for g in range(GS):
                    for r in range(2):
                        last = pe.matmul(out[g], M[0:N, b, r, g, Q + 1:NB, :].rearrange("p n h -> p (n h)"),
                                         Hs[0:N, b, r, g, :], start=(g + r == 0), stop=False, skip_group_check=True)
                last.then_inc(fwd_done, 1)
                for g in range(GS):
                    pe.matmul(out[g], Tz[:, b, g, :], U[:, s, g, NL:2 * NL], start=False, stop=False,
                              skip_group_check=True)
                pe.wait_ge(fwd_done, s + 1)
                for g in range(GS):
                    for r in range(2):
                        last = pe.matmul(out[g], M[N:P, b, r, g, 0:Q, :].rearrange("p n h -> p (n h)"),
                                         Hs[N:P, b, r, g, :], start=False, stop=(g == GS - 1 and r == 1),
                                         skip_group_check=True)
                last.then_inc(y_full, 1)

            for s in range(NSTAGE + 2):
                if s < NSTAGE:
                    two = columns(S0 + 3 * s, T, 2 * T)
                    next(two)
                    if s >= 2:
                        s5_out(s - 2)
                    next(two)
                    n[0] += 4
                    s5_params(s)
                else:
                    s5_out(s - 2)
                if 1 <= s <= NSTAGE:
                    s5_states(s - 1)
                if s < NSTAGE:
                    a = S0 + 3 * s + 2
                    free(a)
                    pe.wait_ge(ada_used, 4 * s + 4)
                    for e in range(2):
                        last = pe.matmul(ps[0:1, a % 2, :], ones[:], ada_acc[:, :, e, :], start=(e == 0), stop=(e == 1))
                    last.then_inc(acc_full, 1)
            pe.wait_ge(z5_in, 16 * 8 * KW)
            for c in range(KW // 2):
                w = unit(pe, n[0])
                n[0] += 1
                for j in range(2):
                    a = L0 + 2 * c + j
                    free(a)
                    for k in range(KW):
                        last = pe.matmul(ps[:, a % 2, 0:T], w[:, k, j * P:(j + 1) * P],
                                         z5[:, k].rearrange("p s c -> p (s c)"), start=(k == 0), stop=(k == KW - 1))
                    last.then_inc(acc_full, 1)
            pe.wait_ge(acc_free, L0 + KW)
            pe.wait_ge(ysb_done, NSTAGE)
            for c in range(D // COLS):
                if c >= 3:
                    pe.wait_ge(fin_used, 3 * (c - 2))
                if c == 0:
                    pe.wait_ge(ya_done, KW)
                    pe.wait_ge(yb_done, KW + 1)
                for x, y in enumerate((ya, yb)):
                    w = unit(pe, n[0])
                    n[0] += 1
                    for j in range(2):
                        for k in range(KW):
                            last = pe.matmul(ps[:, 2 + 2 * (c % 3) + x, j * T:(j + 1) * T], w[:, k, j * P:(j + 1) * P],
                                             y[:, k], start=(k == 0), stop=(k == KW - 1))
                    last.then_inc(fin_full, 1)



def peer(nc, t, ctx, sem, w_ring, ident, mT, units, load_unit, unit, unit_done, out_full, out_used, q_full, q_used,
         mods_dram):
    first = len(units) - 2 * 2 * (D // COLS)
    keep = ExitStack()
    with keep:
        def kb(name, shape, dt=F32):
            return keep.enter_context(nc.sbuf_tensor(name, shape, dt))[(slice(None),) * len(shape)]
        h = kb("h", [P, 2, D])
        f = kb("f", [P, 2, D])
        scores = kb("scores", [P, 2, 2 * HEADS, NKEYS])
        gate2 = kb("gate2", [P, D])
        rss = kb("rss", [P, 8])
        rows_b = sem("rows_b")
        dve2 = sem("dve_step2")
        act2 = sem("act_step2")
        with ExitStack() as st:
            def sb(name, shape, dt=F32):
                return st.enter_context(nc.sbuf_tensor(name, shape, dt))[(slice(None),) * len(shape)]
            ps = st.enter_context(nc.psum_tensor("ps2", [P, 8, 512], F32))[:, :, :]
            r1, r2, r3, r4 = (sb(f"row{i}", [P, D]) for i in range(4))
            fT = sb("fT", [P, KD, T])
            qT = sb("qT", [P, 2, 2, T])
            skn = sb("skn", [P, 2, P])
            skT = sb("skT", [P, 2, P])
            x_in2, sk_in = sem("xres_in"), sem("sk_in")
            rows_c, rows_d = sem("rows_c"), sem("rows_d")
            sq2, f_ready, ft_tr, ft_done, sk_tr, sk_done = (sem("sq2"), sem("f_ready"), sem("ft_tr"), sem("ft_done"),
                                                             sem("sk_tr"), sem("sk_done"))
            h_ready, rinv, rstd2 = sem("h_ready"), sem("rinv"), sem("rstd2")
            sc_full, sc_done, g2_ready = sem("sc_full"), sem("sc_done"), sem("g2_ready")
            row4_free = sem("row4_free")
            block = st.enter_context(nc.Block())

            def bcast(row, m):
                return mods_dram[0:1, m * D:(m + 1) * D].to_broadcast([P, D]) if row is None else row

            @block.sync
            def _(sp):
                for i in range(2):
                    sp.dma_start(h[:, i], t["x"][0, i * P:(i + 1) * P, :]).then_inc(x_in2, 16)
                for u in range(first + RING, len(units)):
                    load_unit(sp, u)

            @block.gpsimd
            def _(pool):
                pool.dma_start(r1[:], mods_dram[0:1, 2 * D:3 * D].to_broadcast([P, D])).then_inc(rows_b, 16)
                pool.dma_start(r2[:], t["b_ada"][0:1, 2 * D:3 * D].to_broadcast([P, D])).then_inc(rows_b, 16)
                pool.dma_start(gate2[:], mods_dram[0:1, 5 * D:6 * D].to_broadcast([P, D])).then_inc(rows_b, 16)
                pool.dma_start(r3[:], t["b_ada"][0:1, 5 * D:6 * D].to_broadcast([P, D])).then_inc(rows_b, 16)
                pool.dma_start(skn[:], t["peer_sub_keys"][0].rearrange("s n c -> n s c")).then_inc(sk_in, 16)
                pool.wait_ge(g2_ready, 1)
                pool.dma_start(r2[:], mods_dram[0:1, 4 * D:5 * D].to_broadcast([P, D])).then_inc(rows_c, 16)
                pool.dma_start(r3[:], t["b_ada"][0:1, 4 * D:5 * D].to_broadcast([P, D])).then_inc(rows_c, 16)
                pool.dma_start(r4[:], t["g_norm2"][0:1, :].to_broadcast([P, D])).then_inc(rows_c, 16)
                pool.wait_ge(row4_free, 1)
                pool.dma_start(r3[:], mods_dram[0:1, 3 * D:4 * D].to_broadcast([P, D])).then_inc(rows_d, 16)
                pool.dma_start(r4[:], t["b_ada"][0:1, 3 * D:4 * D].to_broadcast([P, D])).then_inc(rows_d, 16)

            def scores_out(act, c):
                act.wait_ge(sc_full, c + 1)
                act.activation(scores[:, :, 2 * c:2 * c + 2, :], ps[:, 4 + c % 2, :]
                               .rearrange("p (i j n) -> p i j n", i=2, j=2), ACT.Copy).then_inc(sc_done, 1)

            @block.scalar
            def _(act):
                for i in range(2):
                    act.wait_ge(h_ready, D // COLS)
                    act.activation(fT.rearrange("p k n -> p (k n)")[:, 0:D], h[:, i], ACT.Square,
                                   accum_out=rss[:, i:i + 1]).then_inc(sq2, 1)
                    act.wait_ge(sq2, i + 1)
                act.wait_ge(rinv, 1)
                act.activation(rss[:, 2:4], rss[:, 2:4], ACT.Sqrt).then_inc(rstd2, 1)
                for k in range(KD):
                    act.wait_ge(ft_tr, k + 1)
                    act.activation(fT[:, k, :], ps[:, 2 + k % 2, 0:T], ACT.Copy).then_inc(ft_done, 1)
                for c in range(D // COLS):
                    act.wait_ge(q_full, c + 1)
                    if c >= 2:
                        act.wait_ge(sc_full, c - 1)
                    act.activation(qT[:, c % 2].rearrange("p j n -> p (j n)"), ps[:, c % 2, :], ACT.Copy).then_inc(q_used, 1)
                    if c >= 1:
                        scores_out(act, c - 1)
                scores_out(act, D // COLS - 1)

            @block.vector
            def _(v):
                n = [0]

                def step(ins):
                    n[0] += 1
                    ins.then_inc(dve2, 1)
                    v.wait_ge(dve2, n[0])
                v.wait_ge(rows_b, 16 * 4)
                step(v.tensor_tensor(r1[:], r1[:], r2[:], ALU.add))
                v.tensor_tensor(gate2[:], gate2[:], r3[:], ALU.add).then_inc(g2_ready, 1)
                v.wait_ge(g2_ready, 1)
                v.wait_ge(x_in2, 32)
                v.wait_ge(sk_tr, 1)
                v.tensor_copy(skT[:].rearrange("p s n -> p (s n)"), ps[:, 6, 0:2 * P]).then_inc(sk_done, 1)
                for c in range(D // COLS):
                    v.wait_ge(out_full, c + 1)
                    cols = slice(c * COLS, (c + 1) * COLS)
                    pv = ps[:, c % 2, :].rearrange("p (i n) -> p i n", i=2)
                    tmp = fT[:, 8 + c % 2:10 + c % 2, :]
                    v.tensor_tensor(tmp, pv, r1[:, cols].unsqueeze(1).to_broadcast([P, 2, COLS]), ALU.mult)\
                        .then_inc(out_used, 1)
                    v.wait_ge(out_used, c + 1)
                    v.tensor_tensor(h[:, :, cols], h[:, :, cols], tmp, ALU.add).then_inc(h_ready, 1)
                    v.wait_ge(h_ready, c + 1)
                v.wait_ge(rows_c, 16 * 3)
                step(v.scalar_tensor_tensor(r2[:], r2[:], 1.0, r3[:], ALU.add, ALU.add))
                v.tensor_tensor(r2[:], r2[:], r4[:], ALU.mult).then_inc(row4_free, 1)
                v.wait_ge(row4_free, 1)
                v.wait_ge(sq2, 2)
                step(v.tensor_scalar(rss[:, 2:4], rss[:, 0:2], 1.0 / D, EPS, ALU.mult, ALU.add))
                v.reciprocal(rss[:, 2:4], rss[:, 2:4]).then_inc(rinv, 1)
                v.wait_ge(rows_d, 32)
                step(v.tensor_tensor(r3[:], r3[:], r4[:], ALU.add))
                v.wait_ge(rstd2, 1)
                for i in range(2):
                    step(v.scalar_tensor_tensor(f[:, i], h[:, i], rss[:, 2 + i:3 + i], r2[:], ALU.mult, ALU.mult))
                    v.tensor_tensor(f[:, i], f[:, i], r3[:], ALU.add).then_inc(f_ready, 1)

            @block.tensor
            def _(pe):
                pe.wait_ge(sk_in, 16)
                for s in range(2):
                    last = pe.transpose(ps[:, 6, s * P:(s + 1) * P], skn[:, s], ident[:])
                last.then_inc(sk_tr, 1)
                u = first
                for c in range(D // COLS):
                    w = [unit(pe, u), unit(pe, u + 1)]
                    u += 2
                    if c >= 2:
                        pe.wait_ge(out_used, c - 1)
                    for i in range(2):
                        for k in range(KD):
                            last = pe.matmul(ps[:, c % 2, i * COLS:(i + 1) * COLS], mT[:, k, i * P:(i + 1) * P],
                                             w[k // UK][:, k % UK, :], start=(k == 0), stop=(k == KD - 1))
                            if i == 1 and k == UK - 1:
                                last.then_inc(unit_done, 1)
                    last.then_inc(out_full, 1)
                pe.wait_ge(f_ready, 2)
                for k in range(KD):
                    if k >= 2:
                        pe.wait_ge(ft_done, k - 1)
                    for i in range(2):
                        last = pe.transpose(ps[:, 2 + k % 2, i * P:(i + 1) * P], f[:, i, k * P:(k + 1) * P], ident[:])
                    last.then_inc(ft_tr, 1)
                pe.wait_ge(ft_done, KD)
                pe.wait_ge(sk_done, 1)
                pe.wait_ge(out_used, D // COLS)

                def score(c):
                    pe.wait_ge(q_used, c + 1)
                    if c >= 2:
                        pe.wait_ge(sc_done, c - 1)
                    for i in range(2):
                        for j in range(2):
                            last = pe.matmul(ps[:, 4 + c % 2, (2 * i + j) * P:(2 * i + j + 1) * P],
                                             qT[:, c % 2, j, i * P:(i + 1) * P], skT[:, j], start=True, stop=True)
                    last.then_inc(sc_full, 1)
                for c in range(D // COLS):
                    w = [unit(pe, u), unit(pe, u + 1)]
                    u += 2
                    if c >= 2:
                        pe.wait_ge(q_used, c - 1)
                    for j in range(2):
                        for k in range(KD):
                            last = pe.matmul(ps[:, c % 2, j * T:(j + 1) * T], w[k // UK][:, k % UK, j * P:(j + 1) * P],
                                             fT[:, k, :], start=(k == 0), stop=(k == KD - 1))
                            if j == 1 and k == UK - 1:
                                last.then_inc(unit_done, 1)
                    last.then_inc(q_full, 1)
                    if c >= 1:
                        score(c - 1)
                score(D // COLS - 1)
        experts(nc, t, sem, w_ring, mT, ident, h, f, scores, gate2, rss)


def experts(nc, t, sem, w_ring, mT, ident, h, f, scores, gate2, rss):
    NI = 2 * HEADS
    K = TOPK
    with ExitStack() as st:
        def sb(name, shape, dt=F32):
            return st.enter_context(nc.sbuf_tensor(name, shape, dt))[(slice(None),) * len(shape)]
        ps = st.enter_context(nc.psum_tensor("ps3", [P, 8, 512], F32))[:, :, :]
        ub = [w_ring[:, r].rearrange("p k n -> p (k n)") for r in range(RING)]
        ub += [mT[:, r * KW:(r + 1) * KW, :].rearrange("p k n -> p (k n)") for r in range(2)]
        vb_all = sb("vb", [P, NV, D])
        vb = [vb_all[:, r] for r in range(NV)]
        diag = sb("diag", [P, NDIAG, P])
        iota16 = sb("iota16", [P, K])
        cut = sb("cut", [P, 2, NKEYS])
        sv = sb("sv", [P, 2, K])
        si = sb("si", [P, 2, K], U32)
        sif = sb("sif", [P, 2, K])
        cand = sb("cand", [P, K * K])
        cand2 = sb("cand2", [P, K * K])
        ts = sb("ts", [P, 2, K])
        pos = sb("pos", [P, K], U32)
        pab = sb("pab", [P, 2, K], U32)
        pf = sb("pf", [P, 2, K])
        oh = sb("oh", [P, 2, K, K])
        ef = sb("ef", [P, 3, K])
        eidx = sb("eidx", [P, 3, K], U32)
        sml = sb("sml", [P, 2, 4])
        prob = sb("prob", [P, 2, K])
        hd = sb("hd", [P, 2, K])
        gel = sb("gel", [P, 2, K])
        wgt = sb("wgt", [P, 2, K])
        gf = sb("gf", [P, D])

        iota_ready, idx_ready, top_ready = sem("iota_ready"), sem("idx_ready"), sem("top_ready")
        u_in = [sem(f"urow_in{i}") for i in range(NU)]
        v_in = [sem(f"vrow_in{i}") for i in range(NV)]
        u_used, v_used = sem("urow_used"), sem("vrow_used")
        e_done, dots_done, gel_done, w_ready, diag_done, y_used = (
            sem("e_done"), sem("dots_done"), sem("gel_done"), sem("w_ready"), sem("diag_done"), sem("y_used"))
        gf_in, fin_sq, fin_inv, fin_rstd, fin_done, out_sem = (sem("gf_in"), sem("fin_sq"), sem("fin_inv"),
                                                                sem("fin_rstd"), sem("fin_done"), sem("out_sem"))
        dve3, y_full3 = sem("dve_step3"), sem("y_full3")
        block = st.enter_context(nc.Block())
        iv = lambda i: (i // HEADS, i % HEADS)

        @block.sync
        def _(sp):
            sp.dma_start(gf[:], t["g_final"].rearrange("(a n) -> a n", a=1).to_broadcast([P, D])).then_inc(gf_in, 16)
            for i in range(2):
                sp.wait_ge(fin_done, i + 1)
                sp.dma_start(t["out"][0, i * P:(i + 1) * P, :], h[:, i]).then_inc(out_sem, 16)
            sp.wait_ge(out_sem, 32)

        @block.gpsimd
        def _(pool):
            pool.iota(iota16[:], pattern=[[1, K]], base=0, channel_multiplier=0,
                      allow_small_or_imprecise_dtypes=True).then_inc(iota_ready, 1)

            def gather(i, j, table, ring, n, landed, used, row):
                m = i * K + j
                if m >= n:
                    pool.wait_ge(used, m - n + 1)
                pool.indirect_dma_start(ring[m % n], None, table,
                                        bass.IndirectOffsetOnAxis(ap=eidx[:, i % 3, j:j + 1], axis=0))\
                    .then_inc(landed[m % n], 16)
            tu, tv = t["peer_u"][0], t["peer_v"][0]
            for i in range(NI + 1):
                if i < NI:
                    pool.wait_ge(idx_ready, i + 1)
                for j in range(K):
                    if i < NI:
                        gather(i, j, tu, ub, NU, u_in, u_used, "u")
                    if i >= 1:
                        gather(i - 1, j, tv, vb, NV, v_in, v_used, "v")

        @block.scalar
        def _(act):
            def exps(i):
                act.wait_ge(top_ready, i + 1)
                if i >= 2:
                    act.wait_ge(w_ready, i - 1)
                act.activation(prob[:, i % 2], ts[:, i % 2], ACT.Exp, bias=sml[:, i % 2, 0:1],
                               accum_out=sml[:, i % 2, 1:2]).then_inc(e_done, 1)
            exps(0)
            for i in range(NI):
                if i + 1 < NI:
                    exps(i + 1)
                act.wait_ge(dots_done, i + 1)
                act.activation(gel[:, i % 2], hd[:, i % 2], ACT.Gelu_apprx_tanh).then_inc(gel_done, 1)
                act.wait_ge(w_ready, i + 1)
                for j in range(K):
                    m = i * K + j
                    if m >= NDIAG:
                        act.wait_ge(v_used, m - NDIAG + 1)
                    act.activation(diag[:, m % NDIAG], ident[:], ACT.Copy, scale=wgt[:, i % 2, j:j + 1])\
                        .then_inc(diag_done, 1)
            for i in range(2):
                act.wait_ge(y_used, i + 1)
                act.activation(f[:, i], h[:, i], ACT.Square, accum_out=rss[:, 4 + i:5 + i]).then_inc(fin_sq, 1)
                act.wait_ge(fin_inv, i + 1)
                act.activation(rss[:, 6 + i:7 + i], rss[:, 6 + i:7 + i], ACT.Sqrt).then_inc(fin_rstd, 1)

        @block.vector
        def _(v):
            n = [0]

            def step(ins):
                n[0] += 1
                ins.then_inc(dve3, 1)
                v.wait_ge(dve3, n[0])

            def top16(vals, idx, src, rest):
                step(v.max(vals[:, 0:8], src))
                step(v.max_index(idx[:, 0:8], vals[:, 0:8], src))
                step(v.match_replace(rest, vals[:, 0:8], src, LOWEST))
                step(v.max(vals[:, 8:16], rest))
                step(v.max_index(idx[:, 8:16], vals[:, 8:16], rest))

            def select(i):
                tl, hd_ = iv(i)
                for s in range(2):
                    top16(sv[:, s], si[:, s], scores[:, tl, 2 * hd_ + s, :], cut[:, s])
                step(v.tensor_copy(sif[:], si[:]))
                step(v.tensor_tensor(cand[:].rearrange("p (a b) -> p a b", b=K),
                                     sv[:, 0, :].unsqueeze(2).to_broadcast([P, K, K]),
                                     sv[:, 1, :].unsqueeze(1).to_broadcast([P, K, K]), ALU.add))
                if i >= 2:
                    v.wait_ge(e_done, i - 1)
                top16(ts[:, i % 2], pos[:], cand[:], cand2[:])
                v.tensor_scalar(sml[:, i % 2, 0:1], ts[:, i % 2, 0:1], -1.0, None, ALU.mult).then_inc(top_ready, 1)
                step(v.tensor_scalar(pab[:, 0], pos[:], 4, None, ALU.logical_shift_right))
                step(v.tensor_scalar(pab[:, 1], pos[:], 15, None, ALU.bitwise_and))
                step(v.tensor_copy(pf[:], pab[:]))
                for s in range(2):
                    step(v.tensor_tensor(oh[:, s], iota16[:].unsqueeze(1).to_broadcast([P, K, K]),
                                         pf[:, s].unsqueeze(2).to_broadcast([P, K, K]), ALU.is_equal))
                    step(v.tensor_tensor(oh[:, s], oh[:, s], sif[:, s].unsqueeze(1).to_broadcast([P, K, K]), ALU.mult))
                step(v.tensor_reduce(ef[:, 0:2], oh[:], AX.X, ALU.add))
                step(v.scalar_tensor_tensor(ef[:, 2], ef[:, 0], float(NKEYS), ef[:, 1], ALU.mult, ALU.add))
                if i >= 3:
                    m = (i - 2) * K
                    for r in range(NV):
                        c = (m - 1 - r) // NV + 1
                        v.wait_ge(v_in[(m - 1 - r) % NV], 16 * c)
                v.tensor_copy(eidx[:, i % 3], ef[:, 2]).then_inc(idx_ready, 1)
                v.wait_ge(idx_ready, i + 1)

            def finish(i):
                v.wait_ge(v_used, (i + 1) * HEADS * K)
                v.wait_ge(gf_in, 16)
                acc = ps[:, 4 * i:4 * i + 4, :].rearrange("p c n -> p (c n)")
                step(v.tensor_tensor(f[:, i], acc, gate2[:], ALU.mult))
                v.tensor_tensor(h[:, i], h[:, i], f[:, i], ALU.add).then_inc(y_used, 1)
                v.wait_ge(fin_sq, i + 1)
                step(v.tensor_scalar(rss[:, 6 + i:7 + i], rss[:, 4 + i:5 + i], 1.0 / D, EPS, ALU.mult, ALU.add))
                v.reciprocal(rss[:, 6 + i:7 + i], rss[:, 6 + i:7 + i]).then_inc(fin_inv, 1)
                v.wait_ge(fin_rstd, i + 1)
                v.scalar_tensor_tensor(h[:, i], h[:, i], rss[:, 6 + i:7 + i], gf[:], ALU.mult, ALU.mult)\
                    .then_inc(fin_done, 1)

            v.wait_ge(iota_ready, 1)
            select(0)
            select(1)
            for i in range(NI):
                tl, _h = iv(i)
                if i >= 2:
                    v.wait_ge(gel_done, i - 1)
                for j in range(K):
                    m = i * K + j
                    v.wait_ge(u_in[m % NU], 16 * (m // NU + 1))
                    ins = v.tensor_tensor_reduce(ub[m % NU], ub[m % NU], f[:, tl], 1.0, 0.0, ALU.mult,
                                                 ALU.add, hd[:, i % 2, j:j + 1])
                    ins.then_inc(u_used, 1)
                v.wait_ge(u_used, (i + 1) * K)
                v.wait_ge(e_done, i + 1)
                v.reciprocal(sml[:, i % 2, 2:3], sml[:, i % 2, 1:2]).then_inc(dots_done, 1)
                v.wait_ge(dots_done, i + 1)
                v.wait_ge(gel_done, i + 1)
                if i >= 2:
                    v.wait_ge(diag_done, (i - 1) * K)
                v.scalar_tensor_tensor(wgt[:, i % 2], gel[:, i % 2], sml[:, i % 2, 2:3], prob[:, i % 2],
                                       ALU.mult, ALU.mult).then_inc(w_ready, 1)
                v.wait_ge(w_ready, i + 1)
                if i + 2 < NI:
                    select(i + 2)
            finish(0)
            finish(1)

        @block.tensor
        def _(pe):
            for m in range(NI * K):
                tl, j = m // (HEADS * K), m % (HEADS * K)
                pe.wait_ge(v_in[m % NV], 16 * (m // NV + 1))
                pe.wait_ge(diag_done, m + 1)
                for c in range(D // 512):
                    last = pe.matmul(ps[:, 4 * tl + c, :], diag[:, m % NDIAG], vb[m % NV][:, c * 512:(c + 1) * 512],
                                     start=(j == 0), stop=(j == HEADS * K - 1))
                last.then_inc(v_used, 1)


_INS = ['x', 'c', 'ctx', 'c_ctx', 'w_ada', 'b_ada', 'g_norm1', 'w_in', 's5_a_re', 's5_a_im', 's5_log_dt', 's5_b_re',
        's5_b_im', 's5_c_re', 's5_c_im', 's5_d', 's5_w_glu', 'lru_conv_w', 'lru_conv_b', 'lru_lambda', 'lru_w_r',
        'lru_b_r', 'lru_w_i', 'lru_b_i', 'w_proj_a', 'w_proj_b', 'w_out', 'g_norm2', 'peer_w_query',
        'peer_sub_keys', 'peer_u', 'peer_v', 'g_final']


def kernel(**inputs):
    import concourse.bacc as _bacc
    from concourse.bass_utils import run_bass_kernel_spmd as _run

    nc = _bacc.Bacc("TRN2", target_bir_lowering=False, num_devices=1)
    arrays, aps = {}, {}
    for name in _INS:
        a = np.ascontiguousarray(inputs[name])
        arrays[f"in_{name}"] = a
        aps[name] = nc.dram_tensor(f"in_{name}", a.shape, mybir.dt.from_np(a.dtype), kind="ExternalInput").ap()
    aps["out"] = nc.dram_tensor("out_0", (1, T, D), F32, kind="ExternalOutput").ap()
    build(nc, aps)
    r = _run(nc, [arrays], core_ids=[0])
    return r.results[0]["out_0"]
```

```python
from contextlib import ExitStack

import numpy as np

import concourse.bass as bass
from concourse import mybir

F32 = mybir.dt.float32
U32 = mybir.dt.uint32
ALU = mybir.AluOpType
ACT = mybir.ActivationFunctionType
AX = mybir.AxisListType

P = 128
D = 2048
T = 256
KD = D // P
W = D // 2
KW = W // P
GRID_W = 64
ROWS = T // GRID_W
EPS = 1e-6
LRU_C = 8.0
CONV = 4
G, H, N, Q = 64, 16, 64, 8
NC = 2 * T // Q
NL = T // Q
GS = 4
NSTAGE = G // GS
NB = 2 * Q + 1
COLS = 256
UK = 8
RING = 5
NKEYS, HEADS, TOPK = 128, 8, 16
NV, NDIAG = 5, 6
EARLY_HEADS = 5
TWO_PI_1 = 6.28125
TWO_PI_2 = float(np.float32(round((2 * np.pi - TWO_PI_1) * 2 ** 21) / 2 ** 21))
TWO_PI_3 = float(2 * np.pi - TWO_PI_1 - TWO_PI_2)
PI = float(np.nextafter(np.float32(np.pi), np.float32(0)))
MAGIC = 1.5 * 2 ** 23
LOWEST = -3.0e38

def build(nc, t):
    ctx = ExitStack()
    with ctx:
        def sb(name, shape, dt=F32, stack=ctx):
            return stack.enter_context(nc.sbuf_tensor(name, shape, dt))[(slice(None),) * len(shape)]

        def sem(name):
            return ctx.enter_context(nc.semaphore(name))

        gates_dram = nc.dram_tensor("gates_dram", (2 * KD, P, T), F32, kind="Internal").ap()
        mods_dram = nc.dram_tensor("mods_dram", (2, 6 * D), F32, kind="Internal").ap()
        u_dram = nc.dram_tensor("u_dram", (KW, P, Q, NC), F32, kind="Internal").ap()
        y_dram = nc.dram_tensor("y_dram", (Q, H, G, NL), F32, kind="Internal").ap()

        w_ring = sb("w_ring", [P, RING, UK, COLS])
        ident = sb("ident", [P, P])
        mT = sb("mT", [P, KD, T])

        w_ada = t["w_ada"].rearrange("a (k p) n -> a p k n", p=P)[0]
        w_in = t["w_in"].rearrange("a (k p) n -> a p k n", p=P)[0]
        w_glu = t["s5_w_glu"].rearrange("a (k p) n -> a p k n", p=P)[0]
        w_pa = t["w_proj_a"].rearrange("a (k p) n -> a p k n", p=P)[0]
        w_pb = t["w_proj_b"].rearrange("a (k p) n -> a p k n", p=P)[0]
        w_out = t["w_out"].rearrange("a (k p) n -> a p k n", p=P)[0]
        w_q = t["peer_w_query"].rearrange("a (k p) n -> a p k n", p=P)[0]

        acc_full, acc_free = sem("acc_full"), sem("acc_free")
        unit_done, ada_used = sem("unit_done"), sem("ada_used")
        fin_full, fin_used = sem("fin_full"), sem("fin_used")
        out_full, out_used = sem("out_full"), sem("out_used")
        q_full, q_used = sem("q_full"), sem("q_used")
        w_in_sem = [sem(f"w_landed{i}") for i in range(RING)]

        units = []
        n_done = [0]

        def plan_pair(w, c, s, count):
            n_done[0] += 1
            units.append((w[:, 0:UK, c * COLS:(c + 1) * COLS], unit_done, n_done[0]))
            units.append((w[:, UK:KD, c * COLS:(c + 1) * COLS], s, count))

        acc = 0
        for c in range(16):
            acc += 1
            plan_pair(w_ada, c, acc_full, acc)
        for first in (W // COLS, 0):
            for c in range(W // COLS):
                acc += 2
                plan_pair(w_in, first + c, acc_full, acc)
        for c in range(W // COLS):
            acc += 2
            plan_pair(w_in, 2 * W // COLS + c, acc_full, acc)
        for s in range(NSTAGE):
            acc += 2
            plan_pair(w_in, 3 * W // COLS + s, acc_full, acc)
            acc += 1
            for x in range(4):
                w = w_ada[:, (x % 2) * UK:(x % 2 + 1) * UK]
                c = 16 + 2 * s + x // 2
                units.append((w[:, :, c * COLS:(c + 1) * COLS], ada_used, 4 * s + x + 1))
        for c in range(W // COLS):
            acc += 2
            units.append((w_glu[:, :, c * COLS:(c + 1) * COLS], acc_full, acc))
        NFIN = D // COLS
        for c in range(NFIN):
            units.append((w_pa[:, :, c * COLS:(c + 1) * COLS], fin_full, 2 * c + 1))
            units.append((w_pb[:, :, c * COLS:(c + 1) * COLS], fin_full, 2 * c + 2))
        for c in range(NFIN):
            plan_pair(w_out, c, out_full, c + 1)
        for c in range(NFIN):
            plan_pair(w_q, c, q_full, c + 1)

        def load_unit(eng, u):
            if u >= RING:
                eng.wait_ge(units[u - RING][1], units[u - RING][2])
            eng.dma_start(w_ring[:, u % RING], units[u][0]).then_inc(w_in_sem[u % RING], 16)

        def unit(pe, u):
            pe.wait_ge(w_in_sem[u % RING], 16 * (u // RING + 1))
            return w_ring[:, u % RING]

        mixer(nc, t, ctx, sem, w_ring, ident, mT, units, load_unit, unit, acc_full, acc_free, unit_done,
              ada_used, fin_full, fin_used, mods_dram, u_dram, y_dram, gates_dram)
        peer(nc, t, sem, w_ring, ident, mT, units, load_unit, unit, unit_done,
             out_full, out_used, q_full, q_used, mods_dram)


def stepper(eng, s):
    count = {}

    def link(ins, signal=None):
        x = s if signal is None else signal
        count[id(x)] = count.get(id(x), 0) + 1
        ins.then_inc(x, 1)
        eng.wait_ge(x, count[id(x)])
    return link


def mixer(nc, t, ctx, sem, w_ring, ident, mT, units, load_unit, unit, acc_full, acc_free, unit_done,
          ada_used, fin_full, fin_used, mods_dram, u_dram, y_dram, gates_dram):
    with ExitStack() as st:
        def sb(name, shape, dt=F32):
            return st.enter_context(nc.sbuf_tensor(name, shape, dt))[(slice(None),) * len(shape)]

        ps = st.enter_context(nc.psum_tensor("ps", [P, 8, 512], F32))[:, :, :]

        crow = sb("crow", [2 * KD, P])
        prow = sb("prow", [88, P])
        mrow = sb("mrow", [112, P])
        scol = sb("scol", [P, 2 * KD])
        pcol = sb("pcol", [P, 88])
        mcol = sb("mcol", [P, 112])
        nscale = sb("nscale", [P, 2, KD])
        nshift = sb("nshift", [P, 2, KD])
        modst = sb("modst", [2, 2, 2 * COLS])
        crow_sig = sb("crow_sig", [2 * KD, P])
        nT = sb("nT", [P, KD, 2 * T])
        xss = sb("xss", [P, 8])
        lsm = sb("lsm", [P, 8, 16])
        sp8 = sb("sp8", [P, 16])
        bd = mT[:, 0:KW, :].rearrange("p t (x c) -> p t x c", x=2)
        bd2 = mT[:, KW:KD, :].rearrange("p t (x c) -> p t x c", x=2)
        yl = mT[:, 0:KW, :]
        zu = sb("zu", [P, 2, Q, NC])
        U = nT[:, :, 0:T].rearrange("p k (g c) -> p k g c", g=GS)
        sqt = nT.rearrange("p k n -> p (k n)")[:, 0:D]
        ada_acc = zu.rearrange("p b s c -> p (b s c)").rearrange("p (j e n) -> p j e n", j=2, e=2)
        ones = sb("ones", [P, 1])
        gst = sb("gst", [P, 2, 2, T])
        sm = sb("sm", [P, 20, G])
        pP = sb("pP", [P, 2, G, Q])
        pwb = sb("pwb", [P, 2, G, NB])
        Cc = sb("Cc", [P, 2, G, H])
        Bb = sb("Bb", [P, 2, G, H])
        eb = sb("eb", [P, 2, G, 8])
        ea = sb("ea", [P, 2, G, 8])
        dT = sb("dT", [H, G])
        notfirst = sb("notfirst", [P, NC])
        big = sb("big", [P, 14656])

        xt = [big[:, i * D:(i + 1) * D] for i in range(4)]
        cnat = big[:, 4 * D:4 * D + 2 * KW * P].rearrange("p (r g n) -> p r g n", r=2, g=KW)
        anat = big[0:G, 4 * D + 2048:4 * D + 2048 + 256].rearrange("p (r n) -> p r n", r=2)
        dnat = big[0:G, 4 * D + 2304:4 * D + 2320]
        btmp = big[:, 4 * D + 2320:4 * D + 2320 + 2 * G * H].rearrange("p (r g h) -> p r g h", r=2, g=G)
        pw = big[:, 12560:12560 + 2 * 9 * G].rearrange("p (r g j) -> p r g j", r=2, g=G)
        o = [0]

        def take(n):
            o[0] += n
            return big[:, o[0] - n:o[0]]
        vraw = take(2 * 512).rearrange("p (b n) -> p b n", b=2)
        xc = take(4 * 512).rearrange("p (b n) -> p b n", b=4)
        rt = take(4 * 512).rearrange("p (b d n) -> p b d n", b=2, d=2)
        ig = take(4 * 512).rearrange("p (b d n) -> p b d n", b=2, d=2)
        ag = take(4 * 512).rearrange("p (b d n) -> p b d n", b=2, d=2)
        ltmp = take(2 * 512).rearrange("p (d n) -> p d n", d=2)
        o[0] = 0
        M = take(2 * 2 * GS * NB * H).rearrange("p (b r g n h) -> p b r g n h", b=2, r=2, g=GS, n=NB)
        Mt = take(GS * NB * H).rearrange("p (g n h) -> p g n h", g=GS, n=NB)
        PB = take(2 * GS * P).rearrange("p (r g s h) -> p r g s h", r=2, g=GS, s=Q)
        PBt = take(GS * P).rearrange("p (g s h) -> p g s h", g=GS, s=Q)
        PT = take(2 * 2 * GS * P).rearrange("p (b r g n) -> p b r g n", b=2, r=2, g=GS)
        kst = take(GS * (NB - 2) * H).rearrange("p (g n h) -> p g n h", g=GS, n=NB - 2)
        dg = take(GS * H).rearrange("p (g h) -> p g h", g=GS)
        Tz = take(2 * GS * P).rearrange("p (b g n) -> p b g n", b=2, g=GS)
        rot = take(3 * GS * NC).rearrange("p (x g c) -> p x g c", x=3, g=GS)
        Ssb = take(2 * GS * NC).rearrange("p (r g c) -> p r g c", r=2, g=GS)
        Sr = take(2 * GS * NC).rearrange("p (r g c) -> p r g c", r=2, g=GS)
        St = take(2 * GS * NC).rearrange("p (r g c) -> p r g c", r=2, g=GS)
        Rt = take(2 * GS * NC).rearrange("p (r g c) -> p r g c", r=2, g=GS)
        Hs = take(2 * 2 * GS * NL).rearrange("p (b r g c) -> p b r g c", b=2, r=2, g=GS)
        ysb = take(2 * GS * NL).rearrange("p (b g c) -> p b g c", b=2, g=GS)
        assert o[0] <= 14656, o
        o[0] = 0
        z5 = mT[:, KW:KD, :].rearrange("p k (s c) -> p k s c", s=Q)
        sg = take(2 * T).rearrange("p (b n) -> p b n", b=2)
        ya = take(KW * T).rearrange("p (k n) -> p k n", k=KW)
        yb = take(KW * T).rearrange("p (k n) -> p k n", k=KW)
        sgate = take(2 * 2 * 512).rearrange("p (b x n) -> p b x n", b=2, x=2)
        mt2 = take(2 * 512).rearrange("p (x n) -> p x n", x=2)

        id0, id_ready = sem("id0"), sem("id_ready")
        x_in = [sem(f"x_in{i}") for i in range(4)]
        rows_in, s5_in, b_in = sem("rows_in"), sem("s5_in"), sem("b_in")
        bd_zero, bd_in = sem("bd_zero"), sem("bd_in")
        silu_sig, silu_done, tr_setup, cols_done = sem("silu_sig"), sem("silu_done"), sem("tr_setup"), sem("cols_done")
        tr_s5, s5cols = sem("tr_s5"), sem("s5cols")
        ss_done, ms_done, rstd_done, xn_done = sem("ss_done"), sem("ms_done"), sem("rstd_done"), sem("xn_done")
        dt_done, re_done, tanh_done, th_done, sin_done = (sem("dt_done"), sem("re_done"), sem("tanh_done"),
                                                           sem("th_done"), sem("sin_done"))
        mrow_back = sem("mrow_back")
        fwd_done = sem("fwd_done")
        gst_out, sgate_in = [sem("gst_out0"), sem("gst_out1")], [sem("sgate_in0"), sem("sgate_in1")]
        ada_sum, gt_done = sem("ada_sum"), sem("gt_done")
        labs, lexp, sp_done = sem("labs"), sem("lexp"), sem("sp_done")
        mods_out, mrow_in, mcol_tr, norm_ready = sem("mods_out"), sem("mrow_in"), sem("mcol_tr"), sem("norm_ready")
        nt_tr, nt_ctx, nt_lat = sem("nt_tr"), sem("nt_ctx"), sem("nt_lat")
        conv_done, g_full, g_sig, et_done, q_ready, sq_done, lru_done = (
            sem("conv_done"), sem("g_full"), sem("g_sig"), sem("et_done"), sem("q_ready"), sem("sq_done"),
            sem("lru_done"))
        u_out, u_in, zu_free = sem("u_out"), sem("u_in"), sem("zu_free")
        m_done, pb_done, k_full, kst_done, x_full, pt_done = (sem("m_done"), sem("pb_done"), sem("k_full"),
                                                               sem("kst_done"), sem("x_full"), sem("pt_done"))
        t_in = [sem("t_in0"), sem("t_in1")]
        s_full, ssb_done, h_done, y_full, ysb_done = (sem("s_full"), sem("ssb_done"), sem("h_done"), sem("y_full"),
                                                       sem("ysb_done"))
        y_out, z5_in = [sem("y_out0"), sem("y_out1")], sem("z5_in")
        s5_setup, ssb_read = sem("s5_setup"), sem("ssb_read")
        k_copied, mi_done, rot_done = sem("k_copied"), sem("mi_done"), sem("rot_done")
        yb_done, ya_done = sem("yb_done"), sem("ya_done")
        dve, act_s, pool_s = sem("dve_step"), sem("act_step"), sem("pool_step")

        block = st.enter_context(nc.Block())
        A0, V0, U0, G0 = 0, 16, 24, 32
        S0 = G0 + KW
        L0 = S0 + 3 * NSTAGE
        STAGE_UNITS = 2 * (16 + 8 + 4)
        NUNITS_HERE = STAGE_UNITS + 6 * NSTAGE + 4 + 2 * (D // COLS)

        def toeplitz(sp, s):
            sp.wait_ge(kst_done, s + 1)
            if s >= 2:
                sp.wait_ge(y_full, s - 1)
            kv = kst.rearrange("p g n h -> p g (n h)")
            for i in range(Q):
                sp.dma_start(Tz[i * H:(i + 1) * H, s % 2], kv[0:H, :, (Q - 1 - i) * H:(2 * Q - 1 - i) * H])\
                  .then_inc(t_in[s % 2], 16)

        @block.sync
        def _(sp):
            crow_v = crow[:, :]
            sp.dma_start(crow_v[0:KD], t["c"].rearrange("a (k p) -> (a k) p", p=P)).then_inc(rows_in, 16)
            sp.dma_start(crow_v[KD:2 * KD], t["c_ctx"].rearrange("(k p) -> k p", p=P)).then_inc(rows_in, 16)
            sp.dma_start(prow[0:32], t["lru_conv_w"].rearrange("a w (k p) -> (a w k) p", p=P)).then_inc(rows_in, 16)
            sp.dma_start(prow[32:40], t["lru_conv_b"].rearrange("a (k p) -> (a k) p", p=P)).then_inc(rows_in, 16)
            sp.dma_start(prow[40:56], t["lru_lambda"].rearrange("a d (k p) -> (a d k) p", p=P)).then_inc(rows_in, 16)
            sp.dma_start(prow[56:72], t["lru_b_r"].rearrange("a d (k p) -> (a d k) p", p=P)).then_inc(rows_in, 16)
            sp.dma_start(prow[72:88], t["lru_b_i"].rearrange("a d (k p) -> (a d k) p", p=P)).then_inc(rows_in, 16)
            sp.dma_start(mrow[64:96], t["b_ada"][0, 0:2 * D].rearrange("(k p) -> k p", p=P)).then_inc(mrow_in, 16)
            sp.dma_start(mrow[96:112], t["g_norm1"].rearrange("a (k p) -> (a k) p", p=P)).then_inc(mrow_in, 16)
            for u in range(len(units)):
                if u == NUNITS_HERE + RING:
                    break
                s, x = divmod(u - STAGE_UNITS, 6)
                if x == 5 and 1 <= s <= NSTAGE:
                    toeplitz(sp, s - 1)
                load_unit(sp, u)

        @block.gpsimd
        def _(pool):
            link = stepper(pool, pool_s)
            pool.memset(ident[:], 0.0).then_inc(id0, 1)
            pool.wait_ge(id0, 1)
            pool.affine_select(out=ident[:], in_=ident[:], compare_op=ALU.not_equal, fill=1.0, base=0,
                               pattern=[[-1, P]], channel_multiplier=1).then_inc(id_ready, 1)
            for r, name in enumerate(("s5_a_re", "s5_a_im")):
                pool.dma_start(anat[:, r, :].rearrange("g (d n) -> g d n", d=2),
                               t[name].rearrange("a d g n -> g (a d) n")).then_inc(s5_in, 16)
            for d in range(2):
                src = t["s5_log_dt"][0, d:d + 1, :].to_broadcast([N, G])
                pool.dma_start(sm[d * N:(d + 1) * N, 0, :], src).then_inc(s5_in, 16)
            pool.dma_start(dnat, t["s5_d"].rearrange("a (g h) -> (a g) h", h=H)).then_inc(s5_in, 16)
            for r, name in enumerate(("s5_c_re", "s5_c_im")):
                for d in range(2):
                    pool.dma_start(cnat[:, r, :, d * N:(d + 1) * N],
                                   t[name][0, d].rearrange("(k g) h n -> (g h) k n", g=8)).then_inc(s5_in, 16)
            for r, name in enumerate(("s5_b_re", "s5_b_im")):
                for d in range(2):
                    pool.dma_start(Bb[d * N:(d + 1) * N, r], t[name][0, d].rearrange("g n h -> n g h"))\
                        .then_inc(b_in, 16)
            pool.memset(mT[:], 0.0).then_inc(bd_zero, 1)
            pool.wait_ge(bd_zero, 1)
            for d, dst in enumerate((bd, bd2)):
                for x, name in enumerate(("lru_w_r", "lru_w_i")):
                    src = t[name][0, d].rearrange("(k e) i j -> e i k j", e=2)
                    for e in range(2):
                        pool.dma_start(dst[e * 64:(e + 1) * 64, :, x, e * 64:(e + 1) * 64], src[e])\
                            .then_inc(bd_in, 16)

            def store_mods(q):
                rows = 2 if q < 8 else 1
                pool.wait_ge(acc_free, A0 + 2 * q + 2 if q < 8 else S0 + 3 * (q - 8) + 3)
                pool.dma_start(mods_dram[0:rows, q * 2 * COLS:(q + 1) * 2 * COLS], modst[0:rows, q % 2])\
                    .then_inc(mods_out, 16)
                pool.wait_ge(mods_out, 16 * (q + 1))

            for q in range(8):
                store_mods(q)
            for j, (row, m) in enumerate(((0, 0), (0, 1), (1, 0), (1, 1))):
                pool.dma_start(mrow[16 * j:16 * j + 16], mods_dram[row, m * D:(m + 1) * D]
                               .rearrange("(k p) -> k p", p=P)).then_inc(mrow_back, 16)
            for k in range(KW):
                pool.wait_ge(acc_free, U0 + k + 1)
                pool.dma_start(u_dram[k], zu[:, k % 2]).then_inc(u_out, 16)
                pool.wait_ge(u_out, 16 * (k + 1))
            for s in range(Q):
                for g in range(GS):
                    src = u_dram[:, :, s, :].rearrange("k (a b h) c -> b h (k a) c", h=H, b=GS)[g]
                    pool.dma_start(U[s * H:(s + 1) * H, :, g, :], src).then_inc(u_in, 16)

            def build_pb(s):
                g = slice(s * GS, (s + 1) * GS)
                pr, pi = (pP[:, r, g, :].unsqueeze(3).to_broadcast([P, GS, Q, H]) for r in range(2))
                br, bi = (Bb[:, r, g, :].unsqueeze(2).to_broadcast([P, GS, Q, H]) for r in range(2))
                if s >= 1:
                    pool.wait_ge(x_full, s)
                link(pool.tensor_tensor(PB[:, 0], pr, br, ALU.mult))
                link(pool.tensor_tensor(PBt, pi, bi, ALU.mult))
                link(pool.tensor_tensor(PB[:, 0], PB[:, 0], PBt, ALU.subtract))
                link(pool.tensor_tensor(PB[:, 1], pr, bi, ALU.mult))
                link(pool.tensor_tensor(PBt, pi, br, ALU.mult))
                pool.tensor_tensor(PB[:, 1], PB[:, 1], PBt, ALU.add).then_inc(pb_done, 1)
                pool.wait_ge(pb_done, s + 1)

            def imaginary_product(s):
                if s >= 2:
                    pool.wait_ge(y_full, s - 1)
                g = slice(s * GS, (s + 1) * GS)
                pool.tensor_tensor(M[:, s % 2, 1], pwb[:, 0, g, :].unsqueeze(3).to_broadcast([P, GS, NB, H]),
                                   Cc[:, 1, g, :].unsqueeze(2).to_broadcast([P, GS, NB, H]), ALU.mult)\
                    .then_inc(mi_done, 1)

            def rotations(s):
                if s >= 1:
                    pool.wait_ge(h_done, 4 * s)
                g = slice(s * GS, (s + 1) * GS)
                sh = [P, GS, 8, 8]
                A_ = [ea[:, r, g, :].unsqueeze(3).to_broadcast(sh) for r in range(2)]
                B_ = [eb[:, r, g, :].unsqueeze(2).to_broadcast(sh) for r in range(2)]
                w = [rot[:, x].rearrange("p g (a b) -> p g a b", b=8) for x in range(3)]
                link(pool.tensor_tensor(w[0], A_[0], B_[0], ALU.mult))
                link(pool.tensor_tensor(w[2], A_[1], B_[1], ALU.mult))
                link(pool.tensor_tensor(w[0], w[0], w[2], ALU.subtract))
                link(pool.tensor_tensor(w[1], A_[0], B_[1], ALU.mult))
                link(pool.tensor_tensor(w[2], A_[1], B_[0], ALU.mult))
                link(pool.tensor_tensor(w[1], w[1], w[2], ALU.add))
                for r in range(2):
                    ins = pool.tensor_tensor(Rt[:, r], notfirst[:].unsqueeze(1).to_broadcast([P, GS, NC]),
                                             sm[:, 11, g].unsqueeze(2).to_broadcast([P, GS, NC]), ALU.mult)
                    if r == 0:
                        link(ins)
                    else:
                        ins.then_inc(rot_done, 1)
                        pool.wait_ge(rot_done, s + 1)

            pool.wait_ge(s5_setup, 4)
            pool.wait_ge(lru_done, KW)
            build_pb(0)
            imaginary_product(0)
            imaginary_product(1)
            for s in range(NSTAGE + 2):
                if 2 <= s < NSTAGE:
                    imaginary_product(s)
                if 1 <= s <= NSTAGE:
                    rotations(s - 1)
                if s >= 2:
                    pool.wait_ge(ysb_done, s - 1)
                    r = s - 2
                    pool.dma_start(y_dram[:, :, r * GS:(r + 1) * GS, :].rearrange("s h g c -> (s h) g c"),
                                   ysb[:, r % 2]).then_inc(y_out[r % 2], 16)
                if s < NSTAGE:
                    pool.wait_ge(acc_free, S0 + 3 * s + 2)
                    pool.dma_start(gates_dram[2 * s:2 * s + 2].rearrange("k p n -> p k n"), gst[:, s % 2])\
                        .then_inc(gst_out[s % 2], 16)
                if 1 <= s <= NSTAGE:
                    store_mods(8 + s - 1)
                if s + 1 < NSTAGE:
                    build_pb(s + 1)
            for i in range(2):
                pool.wait_ge(gst_out[i], 16 * NSTAGE // 2)
            pool.wait_ge(acc_free, L0)
            for c in range(D // COLS):
                if c >= 2:
                    pool.wait_ge(fin_used, 3 * (c - 1))
                for x in range(2):
                    pool.dma_start(sgate[:, c % 2, x].rearrange("p (k n) -> p k n", k=2),
                                   gates_dram[x * KD + 2 * c:x * KD + 2 * c + 2].rearrange("k p n -> p k n"))\
                        .then_inc(sgate_in[c % 2], 16)

        @block.scalar
        def _(act):
            link = stepper(act, act_s)
            for i in range(4):
                src = (t["ctx"] if i < 2 else t["x"])[0, (i % 2) * P:(i % 2 + 1) * P, :]
                act.dma_start(xt[i], src).then_inc(x_in[i], 16)
            act.wait_ge(rows_in, 16 * 7)
            act.activation(crow_sig, crow[:, :], ACT.Sigmoid).then_inc(silu_sig, 1)
            for i in range(4):
                act.wait_ge(x_in[i], 16)
                act.activation(sqt, xt[i], ACT.Square, accum_out=xss[:, i:i + 1]).then_inc(ss_done, 1)
                act.wait_ge(ss_done, i + 1)
            act.wait_ge(s5_in, 16 * 9)
            act.activation(sm[:, 1, :], sm[:, 0, :], ACT.Exp).then_inc(dt_done, 1)
            act.wait_ge(labs, 1)
            act.activation(lsm[:, 1], lsm[:, 0], ACT.Exp, scale=-1.0).then_inc(lexp, 1)
            act.wait_ge(re_done, 1)
            act.activation(sm[:, 6, :], sm[:, 4, :], ACT.Tanh, scale=0.5).then_inc(tanh_done, 1)
            act.wait_ge(th_done, 1)
            act.activation(sm[:, 8, :], sm[:, 7, :], ACT.Sin).then_inc(sin_done, 1)
            act.activation(sm[:, 9, :], sm[:, 7, :], ACT.Sin, scale=0.5).then_inc(sin_done, 1)
            act.wait_ge(ms_done, 1)
            act.activation(xss[:, 4:8], xss[:, 4:8], ACT.Sqrt).then_inc(rstd_done, 1)
            act.wait_ge(rstd_done, 1)
            for i in range(4):
                act.activation(xt[i], xt[i], ACT.Copy, scale=xss[:, 4 + i:5 + i]).then_inc(xn_done, 1)

            def mod_rows(a, c):
                act.wait_ge(acc_full, a + 1)
                if c % 2 == 0 and c >= 4:
                    act.wait_ge(mods_out, 16 * (c // 2 - 1))
                act.activation(modst[:, (c // 2) % 2, (c % 2) * COLS:(c % 2 + 1) * COLS], ps[0:2, a % 2, 0:COLS],
                               ACT.Copy).then_inc(acc_free, 1)
            for c in range(16):
                mod_rows(A0 + c, c)
            act.wait_ge(norm_ready, 1)
            for k in range(KD):
                act.wait_ge(nt_tr, k + 1)
                act.activation(nT[:, k, 0:T], ps[:, 2 + k % 2, 0:T], ACT.Identity, scale=nscale[:, 1, k:k + 1],
                               bias=nshift[:, 1, k:k + 1]).then_inc(nt_ctx, 1)

            def gates(k):
                b = k % 2
                if k >= 2:
                    act.wait_ge(lru_done, k - 1)
                for n in range(4):
                    d, x = n // 2, n % 2
                    act.wait_ge(g_full, 4 * k + n + 1)
                    act.activation((rt, ig)[x][:, b, d, :], ps[:, 2 + n, :], ACT.Sigmoid,
                                   bias=pcol[:, 56 + 16 * x + 8 * d + k:57 + 16 * x + 8 * d + k]).then_inc(g_sig, 1)
                act.wait_ge(g_sig, 4 * k + 4)
                for d in range(2):
                    act.activation(ag[:, b, d, :], rt[:, b, d, :], ACT.Exp, scale=lsm[:, 7, 8 * d + k:8 * d + k + 1])\
                        .then_inc(et_done, 1)
                for d in range(2):
                    act.wait_ge(et_done, 4 * k + d + 1)
                    act.activation(rt[:, b, d, :], rt[:, b, d, :], ACT.Tanh, scale=sp8[:, 8 * d + k:8 * d + k + 1])\
                        .then_inc(et_done, 1)

            def roots(k):
                act.wait_ge(q_ready, k + 1)
                for d in range(2):
                    act.activation(rt[:, k % 2, d, :], rt[:, k % 2, d, :], ACT.Sqrt).then_inc(sq_done, 1)

            for i in range(2 * KW):
                act.wait_ge(acc_full, V0 + i + 1)
                if i < KW:
                    if i == 0:
                        act.wait_ge(nt_tr, KD)
                    if i >= 2:
                        act.wait_ge(conv_done, i - 1)
                    link(act.activation(vraw[:, i % 2, 0:T], ps[:, i % 2, 0:T], ACT.Copy))
                    act.activation(vraw[:, i % 2, T:2 * T].rearrange("p (w r) -> p w r", r=ROWS),
                                   ps[:, i % 2, T:2 * T].rearrange("p (r w) -> p w r", w=GRID_W), ACT.Copy)\
                        .then_inc(acc_free, 1)
                else:
                    k = i - KW
                    if k >= 2:
                        act.wait_ge(u_out, 16 * (k - 1))
                    act.activation(zu[:, k % 2], ps[:, i % 2, :].rearrange("p (c s) -> p s c", s=Q), ACT.Copy)\
                        .then_inc(acc_free, 1)
                if 1 <= i <= KW:
                    gates(i - 1)
                if 2 <= i <= KW + 1:
                    roots(i - 2)

            def evac_pt(s):
                act.wait_ge(x_full, s + 1)
                if s >= 2:
                    act.wait_ge(s_full, s - 1)
                act.activation(PT[:, s % 2].rearrange("p r g n -> p r (g n)"), ps[:, 4:6, :], ACT.Copy)\
                    .then_inc(pt_done, 1)

            def evac_kst(s):
                act.wait_ge(k_full, s + 1)
                if s >= 1:
                    act.wait_ge(t_in[(s - 1) % 2], 16 * Q * ((s - 1) // 2 + 1))
                for x in range(2):
                    act.activation(kst[0:H, 2 * x:2 * x + 2].rearrange("p g n h -> p g (n h)"),
                                   ps[0:H, 2 + x, :].rearrange("p (g n) -> p g n", g=2)[:, :, 0:(NB - 2) * H],
                                   ACT.Copy).then_inc(k_copied, 1)

            def evac_s(s):
                act.wait_ge(s_full, s + 1)
                if s >= 1:
                    act.wait_ge(ssb_read, s)
                v = ps[:, 6, :].rearrange("p (x c) -> p x c", c=NC)
                o_ = Ssb.rearrange("p r g c -> p (r g) c")
                act.activation(o_[0:N], v[0:N], ACT.Copy).then_inc(ssb_done, 1)
                for h_ in range(2):
                    c = slice(h_ * NL, (h_ + 1) * NL)
                    act.activation(o_[N:P, :, c], v[N:P, :, c][:, :, ::-1], ACT.Copy).then_inc(ssb_done, 1)

            def evac_y(s):
                act.wait_ge(y_full, s + 1)
                if s >= 2:
                    act.wait_ge(y_out[s % 2], 16 * (s // 2))
                act.activation(ysb[:, s % 2].rearrange("p g c -> p (g c)"), ps[:, 7, 0:GS * NL], ACT.Gelu_apprx_tanh)\
                    .then_inc(ysb_done, 1)

            for k in range(KW):
                act.wait_ge(acc_full, G0 + k + 1)
                if k >= 2:
                    act.wait_ge(yb_done, k - 1)
                act.activation(gst[:, k % 2, 0], ps[:, k % 2, 0:T], ACT.Gelu_apprx_tanh).then_inc(acc_free, 1)

            def gate(s, j):
                a = S0 + 3 * s + j
                act.wait_ge(acc_full, a + 1)
                if s == 0:
                    act.wait_ge(yb_done, KW)
                if s >= 2:
                    act.wait_ge(gst_out[s % 2], 16 * (s // 2))
                act.activation(gst[:, s % 2, j], ps[:, a % 2, 0:T], ACT.Sigmoid).then_inc(acc_free, 1)

            def mod_sums(s):
                a = S0 + 3 * s + 2
                act.wait_ge(acc_full, a + 1)
                act.wait_ge(mods_out, 16 * (8 + s - 1))
                act.activation(modst[0:1, s % 2], ps[0:1, a % 2, :], ACT.Copy).then_inc(acc_free, 1)

            def load_z5(k):
                for i in range(2):
                    act.wait_ge(y_out[i], 16 * (k + 1))
                for g in range(8):
                    act.dma_start(z5[g * H:(g + 1) * H, k], y_dram[:, :, k * 8 + g, :].rearrange("s h c -> h s c"))\
                        .then_inc(z5_in, 16)

            for s in range(NSTAGE + 2):
                if s >= 4 and s % 2 == 0:
                    load_z5(s // 2 - 2)
                if s < NSTAGE:
                    gate(s, 0)
                    gate(s, 1)
                if s >= 2:
                    evac_y(s - 2)
                if s < NSTAGE:
                    evac_kst(s)
                    evac_pt(s)
                if 1 <= s <= NSTAGE:
                    evac_s(s - 1)
                if s < NSTAGE:
                    mod_sums(s)
            load_z5(KW - 1)
            act.wait_ge(h_done, NSTAGE * 4)
            for k in range(KW):
                act.wait_ge(acc_full, L0 + k + 1)
                if k >= 2:
                    act.wait_ge(ya_done, k - 1)
                act.activation(sg[:, k % 2], ps[:, k % 2, 0:T], ACT.Sigmoid).then_inc(acc_free, 1)

        @block.vector
        def _(v):
            v.memset(notfirst[:], 1.0).then_inc(dve, 1)
            steps = [1]
            v.wait_ge(dve, 1)

            def step(ins):
                steps[0] += 1
                ins.then_inc(dve, 1)
                v.wait_ge(dve, steps[0])
            tt, tsc, stt = v.tensor_tensor, v.tensor_scalar, v.scalar_tensor_tensor
            step(v.memset(notfirst[:, 0:1], 0.0))
            step(v.memset(ones[:], 1.0))
            v.wait_ge(silu_sig, 1)
            tt(crow[:], crow[:], crow_sig, ALU.mult).then_inc(silu_done, 1)
            v.wait_ge(tr_setup, 2)
            v.tensor_copy(scol[:], ps[:, 2, 0:32]).then_inc(cols_done, 1)
            step(v.tensor_copy(pcol[:], ps[:, 2, 32:120]))
            lam = pcol[:, 40:56]
            step(tsc(lsm[:, 2], lam, -1.0, None, ALU.mult))
            tt(lsm[:, 0], lam, lsm[:, 2], ALU.max).then_inc(labs, 1)
            v.wait_ge(lexp, 1)
            step(tsc(lsm[:, 3], lsm[:, 1], 2.0, None, ALU.add))
            step(v.reciprocal(lsm[:, 3], lsm[:, 3]))
            step(tt(lsm[:, 3], lsm[:, 3], lsm[:, 1], ALU.mult))
            step(tt(lsm[:, 4], lsm[:, 3], lsm[:, 3], ALU.mult))
            step(tsc(lsm[:, 5], lsm[:, 4], 1.0 / 17, 1.0 / 15, ALU.mult, ALU.add))
            for n in (13, 11, 9, 7, 5, 3, 1):
                step(tt(lsm[:, 5], lsm[:, 5], lsm[:, 4], ALU.mult))
                step(tsc(lsm[:, 5], lsm[:, 5], 1.0 / n, None, ALU.add))
            step(tt(lsm[:, 5], lsm[:, 5], lsm[:, 3], ALU.mult))
            step(tsc(lsm[:, 5], lsm[:, 5], 2.0 * LRU_C, None, ALU.mult))
            step(tsc(lsm[:, 2], lsm[:, 2], 0.0, LRU_C, ALU.max, ALU.mult))
            step(tt(sp8[:], lsm[:, 5], lsm[:, 2], ALU.add))
            tsc(lsm[:, 7], sp8[:], -1.0, None, ALU.mult).then_inc(sp_done, 1)
            v.wait_ge(sp_done, 1)
            v.wait_ge(ss_done, 4)
            step(tsc(xss[:, 4:8], xss[:, 0:4], 1.0 / D, EPS, ALU.mult, ALU.add))
            v.reciprocal(xss[:, 4:8], xss[:, 4:8]).then_inc(ms_done, 1)
            DT, AR, AI, RE, IM, TH, RED, SN, SH = 1, 2, 3, 4, 5, 6, 7, 8, 9
            s_ = lambda i: sm[:, i, :]
            v.wait_ge(tr_s5, 1)
            step(v.tensor_copy(sm[:, AR:AI + 1, :].rearrange("p x g -> p (x g)"), ps[:, 3, 0:2 * G]))
            step(v.tensor_copy(dT[:], ps[0:H, 3, 2 * G:3 * G]))
            v.wait_ge(dt_done, 1)
            step(tt(s_(IM), s_(AI), s_(DT), ALU.mult))
            tt(s_(RE), s_(AR), s_(DT), ALU.mult).then_inc(re_done, 1)
            step(tsc(s_(10), s_(IM), 1.0 / (2 * np.pi), MAGIC, ALU.mult, ALU.add))
            step(tsc(s_(10), s_(10), MAGIC, None, ALU.subtract))
            step(stt(s_(RED), s_(10), -TWO_PI_1, s_(IM), ALU.mult, ALU.add))
            step(stt(s_(RED), s_(10), -TWO_PI_2, s_(RED), ALU.mult, ALU.add))
            step(stt(s_(RED), s_(10), -TWO_PI_3, s_(RED), ALU.mult, ALU.add))
            tsc(s_(RED), s_(RED), PI, -PI, ALU.min, ALU.max).then_inc(th_done, 1)
            v.wait_ge(tanh_done, 1)
            EM, R1, CM, CS, XR, XI, CR, CI, DEN = 10, 11, 12, 13, 14, 15, 16, 17, 18
            step(tsc(s_(R1), s_(TH), -1.0, 1.0, ALU.mult, ALU.add))
            step(v.reciprocal(s_(R1), s_(R1)))
            step(stt(s_(EM), s_(TH), 2.0, s_(R1), ALU.mult, ALU.mult))
            step(tsc(s_(R1), s_(EM), 1.0, None, ALU.add))
            v.wait_ge(sin_done, 2)
            step(stt(s_(CM), s_(SH), -2.0, s_(SH), ALU.mult, ALU.mult))
            step(tsc(s_(CS), s_(CM), 1.0, None, ALU.add))
            step(tt(s_(XR), s_(EM), s_(CS), ALU.mult))
            step(tt(s_(XR), s_(XR), s_(CM), ALU.add))
            step(tt(s_(XI), s_(R1), s_(SN), ALU.mult))
            step(tt(s_(DEN), s_(AR), s_(AR), ALU.mult))
            step(tt(s_(CR), s_(AI), s_(AI), ALU.mult))
            step(tt(s_(DEN), s_(DEN), s_(CR), ALU.add))
            step(v.reciprocal(s_(DEN), s_(DEN)))
            step(tt(s_(CR), s_(XR), s_(AR), ALU.mult))
            step(tt(s_(CI), s_(XI), s_(AI), ALU.mult))
            step(tt(s_(CR), s_(CR), s_(CI), ALU.add))
            step(tt(s_(CR), s_(CR), s_(DEN), ALU.mult))
            step(tt(s_(CI), s_(XI), s_(AR), ALU.mult))
            step(tt(s_(6), s_(XR), s_(AI), ALU.mult))
            step(tt(s_(CI), s_(CI), s_(6), ALU.subtract))
            step(tt(s_(CI), s_(CI), s_(DEN), ALU.mult))

            def cmul(o_re, o_im, ar, ai, br, bi, t1, t2):
                step(tt(t1, ai, bi, ALU.mult))
                step(tt(t2, ar, bi, ALU.mult))
                step(tt(o_re, ar, br, ALU.mult))
                step(tt(o_im, ai, br, ALU.mult))
                step(tt(o_re, o_re, t1, ALU.subtract))
                step(tt(o_im, o_im, t2, ALU.add))

            v.wait_ge(b_in, 16 * 4)
            cr, ci = (s_(x).unsqueeze(2).to_broadcast([P, G, H]) for x in (CR, CI))
            step(tt(btmp[:, 0], ci, Bb[:, 1], ALU.mult))
            step(tt(btmp[:, 1], ci, Bb[:, 0], ALU.mult))
            step(tt(Bb[:, 0], cr, Bb[:, 0], ALU.mult))
            step(tt(Bb[:, 1], cr, Bb[:, 1], ALU.mult))
            step(tt(Bb[:, 0], Bb[:, 0], btmp[:, 0], ALU.subtract))
            step(tt(Bb[:, 1], Bb[:, 1], btmp[:, 1], ALU.add))

            def chain(dst, n, base_re, base_im):
                step(v.memset(dst[:, 0, :, 0:1], 1.0))
                step(v.memset(dst[:, 1, :, 0:1], 0.0))
                step(v.tensor_copy(dst[:, 0, :, 1], base_re))
                step(v.tensor_copy(dst[:, 1, :, 1], base_im))
                for j in range(2, n):
                    cmul(dst[:, 0, :, j], dst[:, 1, :, j], dst[:, 0, :, j - 1], dst[:, 1, :, j - 1], base_re, base_im,
                         s_(6), s_(7))
            step(tsc(s_(XR), s_(XR), 1.0, None, ALU.add))
            chain(pw, 9, s_(XR), s_(XI))
            er, ei = s_(CS), s_(SN)
            nr, ni = s_(8 + 6), s_(8 + 7)
            for i in range(3):
                step(tt(s_(R1), s_(R1), s_(R1), ALU.mult))

            def square(o_re, o_im, a_re, a_im):
                step(tt(s_(6), a_re, a_re, ALU.mult))
                step(tt(s_(7), a_im, a_im, ALU.mult))
                step(stt(o_im, a_re, 2.0, a_im, ALU.mult, ALU.mult))
                step(tt(o_re, s_(6), s_(7), ALU.subtract))
            for i in range(3):
                square(nr, ni, er, ei)
                er, ei, nr, ni = nr, ni, er, ei
            chain(eb, 8, er, ei)
            for i in range(3):
                square(nr, ni, er, ei)
                er, ei, nr, ni = nr, ni, er, ei
            chain(ea, 8, er, ei)
            step(v.memset(pwb[:], 0.0))
            for r in range(2):
                step(v.tensor_copy(pwb[0:N, r, :, Q:NB], pw[0:N, r, :, 0:Q + 1]))
                step(v.tensor_copy(pwb[N:P, r, :, 0:Q + 1], pw[N:P, r, :, ::-1]))
                step(v.tensor_copy(pP[0:N, r], pw[0:N, r, :, 0:Q][:, :, ::-1]))
                step(v.tensor_copy(pP[N:P, r], pw[N:P, r, :, 0:Q]))
            v.wait_ge(tr_s5, 2)
            for b in range(4):
                v.tensor_copy(Cc[:, b // 2, (b % 2) * 32:(b % 2) * 32 + 32, :].rearrange("p g h -> p (g h)"),
                              ps[:, 4 + b, :]).then_inc(s5_setup, 1)
            v.wait_ge(s5_setup, 4)

            v.wait_ge(mcol_tr, 1)
            step(v.tensor_copy(mcol[:], ps[:, 2, 0:112]))
            for x in range(2):
                step(tt(nshift[:, x], mcol[:, 32 * x:32 * x + 16], mcol[:, 64:80], ALU.add))
                step(tt(nscale[:, x], mcol[:, 32 * x + 16:32 * x + 32], mcol[:, 80:96], ALU.add))
                step(tsc(nscale[:, x], nscale[:, x], 1.0, None, ALU.add))
                if x == 0:
                    step(tt(nscale[:, x], nscale[:, x], mcol[:, 96:112], ALU.mult))
                else:
                    tt(nscale[:, x], nscale[:, x], mcol[:, 96:112], ALU.mult).then_inc(norm_ready, 1)
            for k in range(KD):
                v.wait_ge(nt_tr, k + 1)
                tsc(nT[:, k, T:2 * T], ps[:, 4 + k % 2, 0:T], nscale[:, 0, k:k + 1], nshift[:, 0, k:k + 1],
                    ALU.mult, ALU.add).then_inc(nt_lat, 1)

            def conv(k):
                v.wait_ge(acc_free, V0 + k + 1)
                if k >= 4:
                    v.wait_ge(g_full, 4 * (k - 3))
                src, dst = vraw[:, k % 2], xc[:, k % 4]
                cw = [pcol[:, 8 * j + k:8 * j + k + 1] for j in range(CONV)]
                step(tsc(dst, src, cw[1], pcol[:, 32 + k:33 + k], ALU.mult, ALU.add))
                sl, dl = (a[:, T:2 * T].rearrange("p (w r) -> p w r", r=ROWS) for a in (src, dst))
                for j in (0, 2, 3):
                    lo, hi = max(0, 1 - j), max(0, j - 1)
                    step(stt(dst[:, lo:T - hi], src[:, lo + j - 1:T - hi + j - 1], cw[j], dst[:, lo:T - hi],
                             ALU.mult, ALU.add))
                    ins = stt(dl[:, :, lo:ROWS - hi], sl[:, :, lo + j - 1:ROWS - hi + j - 1], cw[j],
                              dl[:, :, lo:ROWS - hi], ALU.mult, ALU.add)
                    if j < 3:
                        step(ins)
                    else:
                        ins.then_inc(conv_done, 1)
                        v.wait_ge(conv_done, k + 1)

            def q_of(k):
                v.wait_ge(et_done, 4 * k + 4)
                b = k % 2
                step(tsc(ltmp, rt[:, b], 1.0, None, ALU.add))
                step(v.reciprocal(ltmp, ltmp))
                stt(rt[:, b], rt[:, b], 2.0, ltmp, ALU.mult, ALU.mult).then_inc(q_ready, 1)
                v.wait_ge(q_ready, k + 1)

            def scans(k):
                b = k % 2
                v.wait_ge(sq_done, 2 * k + 2)
                for d in range(2):
                    step(tt(ig[:, b, d], ig[:, b, d], xc[:, k % 4], ALU.mult))
                    step(tt(ig[:, b, d], ig[:, b, d], rt[:, b, d], ALU.mult))
                fw = (ag[:, b, 0], ig[:, b, 0], rt[:, b, 0])
                step(v.tensor_tensor_scan(fw[2], fw[0], fw[1], 0.0, ALU.mult, ALU.add))
                for lo, first in ((0, 0.0), (T, rt[:, b, 1, 0:1])):
                    a_, b_, h_ = (x[:, b, 1, lo:lo + T][:, ::-1] for x in (ag, ig, rt))
                    step(v.tensor_tensor_scan(h_, a_, b_, first, ALU.mult, ALU.add))
                tt(yl[:, k], rt[:, b, 0, T:2 * T], rt[:, b, 1, T:2 * T], ALU.add).then_inc(lru_done, 1)
                v.wait_ge(lru_done, k + 1)

            for i in range(KW + 3):
                if i < KW:
                    conv(i)
                if 2 <= i <= KW + 1:
                    q_of(i - 2)
                if i >= 3:
                    scans(i - 3)

            def build_m(s):
                b, g = s % 2, slice(s * GS, (s + 1) * GS)
                pr, pi = (pwb[:, r, g, :].unsqueeze(3).to_broadcast([P, GS, NB, H]) for r in range(2))
                c_r, c_i = (Cc[:, r, g, :].unsqueeze(2).to_broadcast([P, GS, NB, H]) for r in range(2))
                if s >= 2:
                    v.wait_ge(y_full, s - 1)
                step(tt(M[:, b, 0], pr, c_r, ALU.mult))
                step(tt(Mt, pi, c_i, ALU.mult))
                step(tt(M[:, b, 0], M[:, b, 0], Mt, ALU.subtract))
                step(tt(Mt, pi, c_r, ALU.mult))
                v.wait_ge(mi_done, s + 1)
                fl = lambda a: a.rearrange("p g n h -> p (g n h)")
                stt(fl(M[:, b, 1]), fl(M[:, b, 1]), -1.0, fl(Mt), ALU.mult, ALU.subtract).then_inc(m_done, 1)
                v.wait_ge(m_done, s + 1)

            def evac_k(s):
                v.wait_ge(k_copied, 2 * s + 2)
                g = slice(s * GS, (s + 1) * GS)
                step(tt(dg[0:H], ident[0:H, 0:H].unsqueeze(1).to_broadcast([H, GS, H]),
                        dT[:, g].unsqueeze(2).to_broadcast([H, GS, H]), ALU.mult))
                tt(kst[0:H, :, Q - 1, :], kst[0:H, :, Q - 1, :], dg[0:H], ALU.add).then_inc(kst_done, 1)
                v.wait_ge(kst_done, s + 1)

            def state_scan(s):
                v.wait_ge(ssb_done, 3 * s + 3)
                v.wait_ge(rot_done, s + 1)
                for r, x in ((0, Sr), (1, St)):
                    ins = tt(x, Ssb, rot[:, r:r + 1].to_broadcast([P, 2, GS, NC]), ALU.mult)
                    if r == 0:
                        step(ins)
                    else:
                        ins.then_inc(ssb_read, 1)
                        v.wait_ge(ssb_read, s + 1)
                step(tt(Sr[:, 0], Sr[:, 0], St[:, 1], ALU.add))
                step(tt(Sr[:, 1], Sr[:, 1], St[:, 0], ALU.subtract))
                fl = lambda a: a.rearrange("p r g c -> p (r g c)")
                step(v.tensor_tensor_scan(fl(St), fl(Rt), fl(Sr), 0.0, ALU.mult, ALU.add))
                c = slice(NL - 1, 2 * NL - 1)
                gc = Sr[:, :, :, 0:NL]
                gs = Sr[:, :, :, NL:2 * NL]
                step(tt(gc, St[:, :, :, c], rot[:, 0:1, :, c].to_broadcast([P, 2, GS, NL]), ALU.mult))
                step(tt(gs, St[:, :, :, c], rot[:, 1:2, :, c].to_broadcast([P, 2, GS, NL]), ALU.mult))
                if s >= 2:
                    v.wait_ge(y_full, s - 1)
                for lo, hi, d in ((0, N, 1), (N, P, -1)):
                    h_ = Hs[lo:hi, s % 2]
                    tt(h_[:, 0, :, ::d], gc[lo:hi, 0], gs[lo:hi, 1], ALU.subtract).then_inc(h_done, 1)
                    tt(h_[:, 1, :, ::d], gc[lo:hi, 1], gs[lo:hi, 0], ALU.add).then_inc(h_done, 1)
                v.wait_ge(h_done, 4 * s + 4)

            def modulations(s, units_of):
                for x in units_of:
                    if x == 0:
                        if s == 0:
                            v.wait_ge(u_out, 16 * KW)
                        else:
                            v.wait_ge(acc_full, S0 + 3 * s)
                    u = STAGE_UNITS + 6 * s + 2 + x
                    w = unit(v, u)
                    for k in range(UK):
                        kk = (x % 2) * UK + k
                        acc_ = ada_acc[:, x // 2, k % 2]
                        ins = (tsc(acc_, w[:, k, :], scol[:, kk:kk + 1], None, ALU.mult) if kk < 2 else
                               stt(acc_, w[:, k, :], scol[:, kk:kk + 1], acc_, ALU.mult, ALU.add))
                        if k == UK - 1:
                            ins.then_inc(ada_used, 1)
                            v.wait_ge(ada_used, 4 * s + x + 1)
                        else:
                            steps[0] += 1
                            ins.then_inc(dve, 1)
                            v.wait_ge(dve, steps[0] - (1 if k else 0))

            for k in range(KW):
                v.wait_ge(acc_free, G0 + k + 1)
                gk = gst[:, k % 2, 0]
                tt(gk.rearrange("p (r w) -> p r w", w=GRID_W), yl[:, k].rearrange("p (w r) -> p r w", r=ROWS),
                   gk.rearrange("p (r w) -> p r w", w=GRID_W), ALU.mult).then_inc(gt_done, 1)
                v.wait_ge(gt_done, k + 1)
                v.tensor_copy(yl[:, k], gk).then_inc(yb_done, 1)
                v.wait_ge(yb_done, k + 1)

            for s in range(NSTAGE + 2):
                if 1 <= s <= NSTAGE:
                    evac_k(s - 1)
                if s >= 2:
                    state_scan(s - 2)
                if s < NSTAGE:
                    modulations(s, (0, 1))
                    build_m(s)
                    modulations(s, (2, 3))
            v.wait_ge(acc_full, L0 + 1)
            v.tensor_copy(yb.rearrange("p k n -> p (k n)"), yl.rearrange("p k n -> p (k n)")).then_inc(yb_done, 1)
            for k in range(KW):
                v.wait_ge(acc_free, L0 + k + 1)
                tt(ya[:, k].rearrange("p (c s) -> p s c", s=Q), z5[:, k],
                   sg[:, k % 2].rearrange("p (s c) -> p s c", s=Q), ALU.mult).then_inc(ya_done, 1)
            for c in range(D // COLS):
                v.wait_ge(sgate_in[c % 2], 32 * (c // 2 + 1))
                for x in range(2):
                    v.wait_ge(fin_full, 2 * c + x + 1)
                    tt(mt2[:, x], sgate[:, c % 2, x], ps[:, 2 + 2 * (c % 3) + x, :], ALU.mult).then_inc(fin_used, 1)
                v.wait_ge(fin_used, 3 * c + 2)
                tt(mT[:, 2 * c:2 * c + 2, :].rearrange("p k n -> p (k n)"), mt2[:, 0], mt2[:, 1], ALU.add)\
                    .then_inc(fin_used, 1)
                v.wait_ge(fin_used, 3 * c + 3)

        @block.tensor
        def _(pe):
            pe.wait_ge(id_ready, 1)
            pe.wait_ge(silu_done, 1)
            pe.transpose(ps[:, 2, 0:32], crow[:], ident[0:32, 0:32]).then_inc(tr_setup, 1)
            pe.transpose(ps[:, 2, 32:120], prow[:], ident[0:88, 0:88]).then_inc(tr_setup, 1)
            pe.wait_ge(s5_in, 16 * 9)
            for r in range(2):
                pe.transpose(ps[:, 3, r * G:(r + 1) * G], anat[:, r], ident[0:G, 0:G])
            pe.transpose(ps[0:H, 3, 2 * G:3 * G], dnat, ident[0:G, 0:G]).then_inc(tr_s5, 1)
            for r in range(2):
                for k in range(KW):
                    last = pe.transpose(ps[:, 4 + 2 * r + k // 4, (k % 4) * P:(k % 4 + 1) * P], cnat[:, r, k], ident[:])
            last.then_inc(tr_s5, 1)
            pe.wait_ge(cols_done, 1)
            sc = scol[:].rearrange("p (j k) -> p k j", j=2)
            n = [0]

            def free(a):
                if a >= 2:
                    pe.wait_ge(acc_free, a - 1)

            def mods(a):
                free(a)
                for h_ in range(2):
                    w = unit(pe, n[0])
                    n[0] += 1
                    for k in range(UK):
                        last = pe.matmul(ps[0:2, a % 2, 0:COLS], sc[:, h_ * UK + k, :], w[:, k, :],
                                         start=(h_ + k == 0), stop=(h_ * UK + k == KD - 1))
                    last.then_inc(unit_done if h_ == 0 else acc_full, 1)

            def columns(a, lo, hi):
                w = [unit(pe, n[0]), unit(pe, n[0] + 1)]
                n[0] += 2
                for j in range(2):
                    free(a + j)
                    for k in range(KD):
                        last = pe.matmul(ps[:, (a + j) % 2, 0:hi - lo], w[k // UK][:, k % UK, j * P:(j + 1) * P],
                                         nT[:, k, lo:hi], start=(k == 0), stop=(k == KD - 1))
                        if j == 1 and k == UK - 1:
                            last.then_inc(unit_done, 1)
                    last.then_inc(acc_full, 1)
                    yield

            for c in range(16):
                mods(A0 + c)
            pe.wait_ge(mrow_in, 16 * 2)
            pe.wait_ge(mrow_back, 16 * 4)
            pe.wait_ge(s5_setup, 4)
            pe.transpose(ps[:, 2, 0:112], mrow[:], ident[0:112, 0:112]).then_inc(mcol_tr, 1)
            pe.wait_ge(xn_done, 4)
            pe.wait_ge(norm_ready, 1)
            for k in range(KD):
                if k >= 2:
                    pe.wait_ge(nt_ctx, k - 1)
                    pe.wait_ge(nt_lat, k - 1)
                for i in range(4):
                    last = pe.transpose(ps[:, 2 + 2 * (i // 2) + k % 2, (i % 2) * P:(i % 2 + 1) * P], xt[i][:, k * P:(k + 1) * P], ident[:])
                last.then_inc(nt_tr, 1)
            pe.wait_ge(nt_ctx, KD)
            pe.wait_ge(nt_lat, KD)
            pe.wait_ge(bd_in, 16 * 8)

            def gates(k):
                pe.wait_ge(conv_done, k + 1)
                if k >= 1:
                    pe.wait_ge(g_sig, 4 * k)
                for i in range(4):
                    pe.matmul(ps[:, 2 + i, :], (bd, bd2)[i // 2][:, k, i % 2, :], xc[:, k % 4], start=True, stop=True)\
                        .then_inc(g_full, 1)

            i = 0
            for c in range(2 * KW // 2):
                for _ in columns(V0 + 2 * c, 0, 2 * T):
                    if 1 <= i <= KW:
                        gates(i - 1)
                    i += 1

            for c in range(KW // 2):
                for _ in columns(G0 + 2 * c, T, 2 * T):
                    pass

            def s5_params(s):
                b = s % 2
                pe.wait_ge(m_done, s + 1)
                if s >= 1:
                    pe.wait_ge(kst_done, s)
                else:
                    pe.wait_ge(g_sig, 4 * KW)
                for g in range(GS):
                    for r in range(2):
                        last = pe.matmul(ps[0:H, 2 + g // 2, (g % 2) * 256:(g % 2) * 256 + (NB - 2) * H],
                                         Bb[:, r, s * GS + g, :],
                                         M[:, b, r, g, 1:NB - 1, :].rearrange("p n h -> p (n h)"),
                                         start=(r == 0), stop=(r == 1))
                last.then_inc(k_full, 1)
                pe.wait_ge(pb_done, s + 1)
                if s >= 1:
                    pe.wait_ge(pt_done, s)
                for r in range(2):
                    for g in range(GS):
                        last = pe.transpose(ps[:, 4 + r, g * P:(g + 1) * P], PB[:, r, g].rearrange("p s h -> p (s h)"),
                                            ident[:])
                last.then_inc(x_full, 1)

            def s5_states(s):
                pe.wait_ge(pt_done, s + 1)
                pe.wait_ge(u_in, 16 * Q * GS)
                if s >= 1:
                    pe.wait_ge(ssb_done, 3 * s)
                for r in range(2):
                    for g in range(GS):
                        last = pe.matmul(ps[:, 6, (r * GS + g) * NC:(r * GS + g + 1) * NC], PT[:, s % 2, r, g, :],
                                         U[:, s, g, :], start=True, stop=True)
                last.then_inc(s_full, 1)

            def s5_out(s):
                b = s % 2
                pe.wait_ge(t_in[b], 16 * Q * (s // 2 + 1))
                pe.wait_ge(h_done, 4 * s + 4)
                if s >= 1:
                    pe.wait_ge(ysb_done, s)
                out = [ps[:, 7, g * NL:(g + 1) * NL] for g in range(GS)]
                for g in range(GS):
                    for r in range(2):
                        last = pe.matmul(out[g], M[0:N, b, r, g, Q + 1:NB, :].rearrange("p n h -> p (n h)"),
                                         Hs[0:N, b, r, g, :], start=(g + r == 0), stop=False, skip_group_check=True)
                last.then_inc(fwd_done, 1)
                for g in range(GS):
                    pe.matmul(out[g], Tz[:, b, g, :], U[:, s, g, NL:2 * NL], start=False, stop=False,
                              skip_group_check=True)
                pe.wait_ge(fwd_done, s + 1)
                for g in range(GS):
                    for r in range(2):
                        last = pe.matmul(out[g], M[N:P, b, r, g, 0:Q, :].rearrange("p n h -> p (n h)"),
                                         Hs[N:P, b, r, g, :], start=False, stop=(g == GS - 1 and r == 1),
                                         skip_group_check=True)
                last.then_inc(y_full, 1)

            for s in range(NSTAGE + 2):
                if s < NSTAGE:
                    two = columns(S0 + 3 * s, T, 2 * T)
                    next(two)
                    if s >= 2:
                        s5_out(s - 2)
                    next(two)
                    n[0] += 4
                    s5_params(s)
                else:
                    s5_out(s - 2)
                if 1 <= s <= NSTAGE:
                    s5_states(s - 1)
                if s < NSTAGE:
                    a = S0 + 3 * s + 2
                    free(a)
                    pe.wait_ge(ada_used, 4 * s + 4)
                    for e in range(2):
                        last = pe.matmul(ps[0:1, a % 2, :], ones[:], ada_acc[:, :, e, :], start=(e == 0), stop=(e == 1))
                    last.then_inc(acc_full, 1)
            pe.wait_ge(z5_in, 16 * 8 * KW)
            for c in range(KW // 2):
                w = unit(pe, n[0])
                n[0] += 1
                for j in range(2):
                    a = L0 + 2 * c + j
                    free(a)
                    for k in range(KW):
                        last = pe.matmul(ps[:, a % 2, 0:T], w[:, k, j * P:(j + 1) * P],
                                         z5[:, k].rearrange("p s c -> p (s c)"), start=(k == 0), stop=(k == KW - 1))
                    last.then_inc(acc_full, 1)
            pe.wait_ge(acc_free, L0 + KW)
            pe.wait_ge(ysb_done, NSTAGE)
            for c in range(D // COLS):
                if c >= 3:
                    pe.wait_ge(fin_used, 3 * (c - 2))
                if c == 0:
                    pe.wait_ge(ya_done, KW)
                    pe.wait_ge(yb_done, KW + 1)
                for x, y in enumerate((ya, yb)):
                    w = unit(pe, n[0])
                    n[0] += 1
                    for j in range(2):
                        for k in range(KW):
                            last = pe.matmul(ps[:, 2 + 2 * (c % 3) + x, j * T:(j + 1) * T], w[:, k, j * P:(j + 1) * P],
                                             y[:, k], start=(k == 0), stop=(k == KW - 1))
                    last.then_inc(fin_full, 1)



def peer(nc, t, sem, w_ring, ident, mT, units, load_unit, unit, unit_done, out_full, out_used, q_full, q_used,
         mods_dram):
    first = len(units) - 2 * 2 * (D // COLS)
    NCH = D // COLS
    NI = 2 * HEADS
    K = TOPK
    with ExitStack() as st:
        def sb(name, shape, dt=F32):
            return st.enter_context(nc.sbuf_tensor(name, shape, dt))[(slice(None),) * len(shape)]
        ps = st.enter_context(nc.psum_tensor("ps2", [P, 8, 512], F32))[:, :, :]
        h = sb("h", [P, 2, D])
        f = sb("f", [P, 2, D])
        fT = sb("fT", [P, KD, T])
        scores = sb("scores", [P, 2, 2 * HEADS, NKEYS])
        rows = sb("rows", [P, 4, D])
        vb_all = sb("vb", [P, NV, D])
        rss = sb("rss", [P, 8])
        ssq = sb("ssq", [P, 2, NCH])
        qT = sb("qT", [P, 2, T])
        skT = sb("skT", [P, 2, P])
        diag = sb("diag", [P, NDIAG, P])
        iota16 = sb("iota16", [P, K])
        cut = sb("cut", [P, 2, NKEYS])
        skn = cut
        sv = sb("sv", [P, 2, K])
        si = sb("si", [P, 2, K], U32)
        sif = sb("sif", [P, 2, K])
        cand = sb("cand", [P, K * K])
        cand2 = sb("cand2", [P, K * K])
        ts = sb("ts", [P, 2, K])
        pos = sb("pos", [P, K], U32)
        pab = sb("pab", [P, 2, K], U32)
        pf = sb("pf", [P, 2, K])
        oh = sb("oh", [P, 2, K, K])
        ef = sb("ef", [P, 3, K])
        eidx = sb("eidx", [P, 3, K], U32)
        sml = sb("sml", [P, 2, 4])
        prob = sb("prob", [P, 2, K])
        hd = sb("hd", [P, 2, K])
        gel = sb("gel", [P, 2, K])
        wgt = sb("wgt", [P, 2, K])

        gate1, gate1_b, scale2, scale2_b = (rows[:, r] for r in range(4))
        norm2, shift2, shift2_b = (vb_all[:, r] for r in range(3))
        ub = [mT[:, r * KW:(r + 1) * KW, :].rearrange("p k n -> p (k n)") for r in range(2)]
        ub += [rows[:, r] for r in range(4)]
        vb = [vb_all[:, r] for r in range(NV)]
        gf, gate2, gate2_b = (w_ring[:, r].rearrange("p k n -> p (k n)") for r in range(3))

        x_in2, sk_in = sem("xres_in"), sem("sk_in")
        gate1_in, rows_in2, last_rows_in = sem("gate1_in"), sem("rows_in2"), sem("last_rows_in")
        gate1_ready, tmp_done, hr_done, h_ready = sem("gate1_ready"), sem("tmp_done"), sem("hr_done"), sem("h_ready")
        sq2, rinv, rstd2, f_ready, ft_tr, ft_done = (sem("sq2"), sem("rinv"), sem("rstd2"), sem("f_ready"),
                                                     sem("ft_tr"), sem("ft_done"))
        sk_tr, sk_done, sc_full, sc_done = sem("sk_tr"), sem("sk_done"), sem("sc_full"), sem("sc_done")
        iota_ready, idx_ready, top_ready = sem("iota_ready"), sem("idx_ready"), sem("top_ready")
        u_in = [sem(f"urow_in{i}") for i in range(len(ub))]
        v_in = [sem(f"vrow_in{i}") for i in range(NV)]
        u_used, v_used = sem("urow_used"), sem("vrow_used")
        e_done, dots_done, gel_done, w_ready, diag_done, y_used = (
            sem("e_done"), sem("dots_done"), sem("gel_done"), sem("w_ready"), sem("diag_done"), sem("y_used"))
        fin_sq, fin_inv, fin_rstd, fin_done, out_sem = (sem("fin_sq"), sem("fin_inv"), sem("fin_rstd"),
                                                        sem("fin_done"), sem("out_sem"))
        dve3 = sem("dve_step3")
        block = st.enter_context(nc.Block())

        @block.sync
        def _(sp):
            for i in range(2):
                sp.dma_start(h[:, i], t["x"][0, i * P:(i + 1) * P, :]).then_inc(x_in2, 16)
            for u in range(first + RING, len(units)):
                load_unit(sp, u)
            sp.wait_ge(q_full, NCH)
            sp.dma_start(gf, t["g_final"].rearrange("(a n) -> a n", a=1).to_broadcast([P, D])).then_inc(last_rows_in, 16)
            sp.dma_start(gate2, mods_dram[0:1, 5 * D:6 * D].to_broadcast([P, D])).then_inc(last_rows_in, 16)
            sp.dma_start(gate2_b, t["b_ada"][0:1, 5 * D:6 * D].to_broadcast([P, D])).then_inc(last_rows_in, 16)
            for i in range(2):
                sp.wait_ge(fin_done, i + 1)
                sp.dma_start(t["out"][0, i * P:(i + 1) * P, :], h[:, i]).then_inc(out_sem, 16)
            sp.wait_ge(out_sem, 32)

        @block.gpsimd
        def _(pool):
            pool.dma_start(gate1, mods_dram[0:1, 2 * D:3 * D].to_broadcast([P, D])).then_inc(gate1_in, 16)
            pool.dma_start(gate1_b, t["b_ada"][0:1, 2 * D:3 * D].to_broadcast([P, D])).then_inc(gate1_in, 16)
            pool.dma_start(skn[:], t["peer_sub_keys"][0].rearrange("s n c -> n s c")).then_inc(sk_in, 16)
            pool.dma_start(scale2, mods_dram[0:1, 4 * D:5 * D].to_broadcast([P, D])).then_inc(rows_in2, 16)
            pool.dma_start(scale2_b, t["b_ada"][0:1, 4 * D:5 * D].to_broadcast([P, D])).then_inc(rows_in2, 16)
            pool.dma_start(norm2, t["g_norm2"][0:1, :].to_broadcast([P, D])).then_inc(rows_in2, 16)
            pool.dma_start(shift2, mods_dram[0:1, 3 * D:4 * D].to_broadcast([P, D])).then_inc(rows_in2, 16)
            pool.dma_start(shift2_b, t["b_ada"][0:1, 3 * D:4 * D].to_broadcast([P, D])).then_inc(rows_in2, 16)
            pool.iota(iota16[:], pattern=[[1, K]], base=0, channel_multiplier=0,
                      allow_small_or_imprecise_dtypes=True).then_inc(iota_ready, 1)

            def gather(i, j, table, ring, landed, used):
                m = i * K + j
                n = len(ring)
                if m >= n:
                    pool.wait_ge(used, m - n + 1)
                pool.indirect_dma_start(ring[m % n], None, table,
                                        bass.IndirectOffsetOnAxis(ap=eidx[:, i % 3, j:j + 1], axis=0))\
                    .then_inc(landed[m % n], 16)
            tu, tv = t["peer_u"][0], t["peer_v"][0]
            for i in range(NI + 1):
                if i < NI:
                    pool.wait_ge(idx_ready, i + 1)
                for j in range(K):
                    if i < NI:
                        gather(i, j, tu, ub, u_in, u_used)
                    if i >= 1:
                        gather(i - 1, j, tv, vb, v_in, v_used)

        @block.scalar
        def _(act):
            for c in range(NCH):
                act.wait_ge(h_ready, c + 1)
                for i in range(2):
                    if c + i:
                        act.wait_ge(sq2, 2 * c + i)
                    act.activation(fT[:, 0, 0:COLS], h[:, i, c * COLS:(c + 1) * COLS], ACT.Square,
                                   accum_out=ssq[:, i, c:c + 1]).then_inc(sq2, 1)
            act.wait_ge(rinv, 1)
            act.activation(rss[:, 2:4], rss[:, 2:4], ACT.Sqrt).then_inc(rstd2, 1)
            for k in range(KD // 2):
                act.wait_ge(ft_tr, k + 1)
                if k == 0:
                    act.wait_ge(sq2, 2 * NCH)
                act.activation(fT[:, 2 * k:2 * k + 2, :].rearrange("p k n -> p (k n)"), ps[:, 2 + k % 2, :],
                               ACT.Copy).then_inc(ft_done, 1)

            def query_out(c):
                act.wait_ge(q_full, c + 1)
                if c >= 1:
                    act.wait_ge(sc_full, c)
                act.activation(qT.rearrange("p j n -> p (j n)"), ps[:, 4 + c % 2, :], ACT.Copy).then_inc(q_used, 1)
                act.wait_ge(sc_full, c + 1)
                act.activation(scores[:, :, 2 * c:2 * c + 2, :], ps[:, 6 + c % 2, :]
                               .rearrange("p (i j n) -> p i j n", i=2, j=2), ACT.Copy).then_inc(sc_done, 1)

            def exps(i):
                act.wait_ge(top_ready, i + 1)
                if i >= 2:
                    act.wait_ge(w_ready, i - 1)
                act.activation(prob[:, i % 2], ts[:, i % 2], ACT.Exp, bias=sml[:, i % 2, 0:1],
                               accum_out=sml[:, i % 2, 1:2]).then_inc(e_done, 1)

            def final_squares(i):
                act.wait_ge(y_used, i + 1)
                act.activation(f[:, i], h[:, i], ACT.Square, accum_out=rss[:, 4 + i:5 + i]).then_inc(fin_sq, 1)

            def final_root(i):
                act.wait_ge(fin_inv, i + 1)
                act.activation(rss[:, 6 + i:7 + i], rss[:, 6 + i:7 + i], ACT.Sqrt).then_inc(fin_rstd, 1)

            for c in range(EARLY_HEADS):
                query_out(c)
            exps(0)
            for i in range(NI):
                if i + 1 < NI:
                    exps(i + 1)
                act.wait_ge(dots_done, i + 1)
                act.activation(gel[:, i % 2], hd[:, i % 2], ACT.Gelu_apprx_tanh).then_inc(gel_done, 1)
                if i == HEADS + 2:
                    final_squares(0)
                if i == HEADS + 3:
                    final_root(0)
                act.wait_ge(w_ready, i + 1)
                for j in range(K):
                    m = i * K + j
                    if j == K // 2 and EARLY_HEADS + i < HEADS:
                        query_out(EARLY_HEADS + i)
                    if m >= NDIAG:
                        act.wait_ge(v_used, m - NDIAG + 1)
                    act.activation(diag[:, m % NDIAG], ident[:], ACT.Copy, scale=wgt[:, i % 2, j:j + 1])\
                        .then_inc(diag_done, 1)
            final_squares(1)
            final_root(1)

        @block.vector
        def _(v):
            n = [0]

            def step(ins):
                n[0] += 1
                ins.then_inc(dve3, 1)
                v.wait_ge(dve3, n[0])

            v.wait_ge(gate1_in, 32)
            v.tensor_tensor(gate1, gate1, gate1_b, ALU.add).then_inc(gate1_ready, 1)
            v.wait_ge(sk_tr, 1)
            v.tensor_copy(skT[:].rearrange("p s n -> p (s n)"), ps[:, 6, 0:2 * P]).then_inc(sk_done, 1)
            v.wait_ge(rows_in2, 16 * 5)
            step(v.scalar_tensor_tensor(scale2, scale2, 1.0, scale2_b, ALU.add, ALU.add))
            step(v.tensor_tensor(scale2, scale2, norm2, ALU.mult))
            step(v.tensor_tensor(shift2, shift2, shift2_b, ALU.add))
            v.wait_ge(x_in2, 32)
            v.wait_ge(gate1_ready, 1)
            for c in range(NCH):
                v.wait_ge(out_full, c + 1)
                cols = slice(c * COLS, (c + 1) * COLS)
                pv = ps[:, c % 2, :].rearrange("p (i n) -> p i n", i=2)
                tmp = fT[:, 8 + 2 * (c % 2):10 + 2 * (c % 2), :]
                v.tensor_tensor(tmp, pv, gate1[:, cols].unsqueeze(1).to_broadcast([P, 2, COLS]), ALU.mult)\
                    .then_inc(out_used, 1)
                v.wait_ge(out_used, c + 1)
                v.tensor_tensor(h[:, :, cols], h[:, :, cols], tmp, ALU.add).then_inc(h_ready, 1)
                v.wait_ge(h_ready, c + 1)
                v.tensor_tensor(f[:, :, cols], h[:, :, cols], scale2[:, cols].unsqueeze(1).to_broadcast([P, 2, COLS]),
                                ALU.mult).then_inc(hr_done, 1)
            v.wait_ge(sq2, 2 * NCH)
            step(v.tensor_reduce(rss[:, 0:2], ssq[:], AX.X, ALU.add))
            step(v.tensor_scalar(rss[:, 2:4], rss[:, 0:2], 1.0 / D, EPS, ALU.mult, ALU.add))
            v.reciprocal(rss[:, 2:4], rss[:, 2:4]).then_inc(rinv, 1)
            v.wait_ge(hr_done, NCH)
            v.wait_ge(rstd2, 1)
            for c in range(D // 512):
                cols = slice(c * 512, (c + 1) * 512)
                for i in range(2):
                    v.scalar_tensor_tensor(f[:, i, cols], f[:, i, cols], rss[:, 2 + i:3 + i], shift2[:, cols],
                                           ALU.mult, ALU.add).then_inc(f_ready, 1)
            v.wait_ge(f_ready, 2 * (D // 512))

            def top16(vals, idx, src, rest):
                step(v.max(vals[:, 0:8], src))
                step(v.max_index(idx[:, 0:8], vals[:, 0:8], src))
                step(v.match_replace(rest, vals[:, 0:8], src, LOWEST))
                step(v.max(vals[:, 8:16], rest))
                step(v.max_index(idx[:, 8:16], vals[:, 8:16], rest))

            def select(i):
                tile, head = divmod(i, HEADS)
                v.wait_ge(sc_done, head + 1)
                for s in range(2):
                    top16(sv[:, s], si[:, s], scores[:, tile, 2 * head + s, :], cut[:, s])
                step(v.tensor_copy(sif[:], si[:]))
                step(v.tensor_tensor(cand[:].rearrange("p (a b) -> p a b", b=K),
                                     sv[:, 0, :].unsqueeze(2).to_broadcast([P, K, K]),
                                     sv[:, 1, :].unsqueeze(1).to_broadcast([P, K, K]), ALU.add))
                if i >= 2:
                    v.wait_ge(e_done, i - 1)
                top16(ts[:, i % 2], pos[:], cand[:], cand2[:])
                v.tensor_scalar(sml[:, i % 2, 0:1], ts[:, i % 2, 0:1], -1.0, None, ALU.mult).then_inc(top_ready, 1)
                step(v.tensor_scalar(pab[:, 0], pos[:], 4, None, ALU.logical_shift_right))
                step(v.tensor_scalar(pab[:, 1], pos[:], 15, None, ALU.bitwise_and))
                step(v.tensor_copy(pf[:], pab[:]))
                for s in range(2):
                    step(v.tensor_tensor(oh[:, s], iota16[:].unsqueeze(1).to_broadcast([P, K, K]),
                                         pf[:, s].unsqueeze(2).to_broadcast([P, K, K]), ALU.is_equal))
                    step(v.tensor_tensor(oh[:, s], oh[:, s], sif[:, s].unsqueeze(1).to_broadcast([P, K, K]), ALU.mult))
                step(v.tensor_reduce(ef[:, 0:2], oh[:], AX.X, ALU.add))
                step(v.scalar_tensor_tensor(ef[:, 2], ef[:, 0], float(NKEYS), ef[:, 1], ALU.mult, ALU.add))
                if i >= 3:
                    m = (i - 2) * K
                    for r in range(min(NV, K)):
                        v.wait_ge(v_in[(m - 1 - r) % NV], 16 * ((m - 1 - r) // NV + 1))
                v.tensor_copy(eidx[:, i % 3], ef[:, 2]).then_inc(idx_ready, 1)
                v.wait_ge(idx_ready, i + 1)

            def add_experts(i):
                v.wait_ge(v_used, (i + 1) * HEADS * K)
                acc = ps[:, 4 * i:4 * i + 4, :].rearrange("p c n -> p (c n)")
                step(v.tensor_tensor(f[:, i], acc, gate2, ALU.mult))
                v.tensor_tensor(h[:, i], h[:, i], f[:, i], ALU.add).then_inc(y_used, 1)

            def final_inverse(i):
                v.wait_ge(fin_sq, i + 1)
                step(v.tensor_scalar(rss[:, 6 + i:7 + i], rss[:, 4 + i:5 + i], 1.0 / D, EPS, ALU.mult, ALU.add))
                v.reciprocal(rss[:, 6 + i:7 + i], rss[:, 6 + i:7 + i]).then_inc(fin_inv, 1)

            def final_scale(i):
                v.wait_ge(fin_rstd, i + 1)
                v.scalar_tensor_tensor(h[:, i], h[:, i], rss[:, 6 + i:7 + i], gf, ALU.mult, ALU.mult)\
                    .then_inc(fin_done, 1)

            v.wait_ge(iota_ready, 1)
            select(0)
            select(1)
            for i in range(NI):
                if i >= 2:
                    v.wait_ge(gel_done, i - 1)
                for j in range(K):
                    m = i * K + j
                    n_u = len(ub)
                    v.wait_ge(u_in[m % n_u], 16 * (m // n_u + 1))
                    v.tensor_tensor_reduce(ub[m % n_u], ub[m % n_u], f[:, i // HEADS], 1.0, 0.0, ALU.mult,
                                           ALU.add, hd[:, i % 2, j:j + 1]).then_inc(u_used, 1)
                v.wait_ge(u_used, (i + 1) * K)
                v.wait_ge(e_done, i + 1)
                v.reciprocal(sml[:, i % 2, 2:3], sml[:, i % 2, 1:2]).then_inc(dots_done, 1)
                v.wait_ge(dots_done, i + 1)
                v.wait_ge(gel_done, i + 1)
                if i >= 2:
                    v.wait_ge(diag_done, (i - 1) * K)
                v.scalar_tensor_tensor(wgt[:, i % 2], gel[:, i % 2], sml[:, i % 2, 2:3], prob[:, i % 2],
                                       ALU.mult, ALU.mult).then_inc(w_ready, 1)
                v.wait_ge(w_ready, i + 1)
                if i + 2 < NI:
                    select(i + 2)
                if i == HEADS + 1:
                    v.wait_ge(last_rows_in, 48)
                    step(v.tensor_tensor(gate2, gate2, gate2_b, ALU.add))
                    add_experts(0)
                if i == HEADS + 2:
                    final_inverse(0)
                if i == HEADS + 3:
                    final_scale(0)
            add_experts(1)
            final_inverse(1)
            final_scale(1)

        @block.tensor
        def _(pe):
            pe.wait_ge(sk_in, 16)
            for s in range(2):
                last = pe.transpose(ps[:, 6, s * P:(s + 1) * P], skn[:, s], ident[:])
            last.then_inc(sk_tr, 1)
            for c in range(NCH):
                w = [unit(pe, first + 2 * c), unit(pe, first + 2 * c + 1)]
                if c >= 2:
                    pe.wait_ge(out_used, c - 1)
                for i in range(2):
                    for k in range(KD):
                        last = pe.matmul(ps[:, c % 2, i * COLS:(i + 1) * COLS], mT[:, k, i * P:(i + 1) * P],
                                         w[k // UK][:, k % UK, :], start=(k == 0), stop=(k == KD - 1))
                        if i == 1 and k == UK - 1:
                            last.then_inc(unit_done, 1)
                last.then_inc(out_full, 1)
            for k in range(KD):
                pe.wait_ge(f_ready, 2 * (k // 4 + 1))
                if k >= 4 and k % 2 == 0:
                    pe.wait_ge(ft_done, k // 2 - 1)
                for i in range(2):
                    last = pe.transpose(ps[:, 2 + k // 2 % 2, (k % 2) * T + i * P:(k % 2) * T + (i + 1) * P],
                                        f[:, i, k * P:(k + 1) * P], ident[:])
                if k % 2 == 1:
                    last.then_inc(ft_tr, 1)
            pe.wait_ge(sk_done, 1)

            def query(c):
                w = [unit(pe, first + 2 * (NCH + c)), unit(pe, first + 2 * (NCH + c) + 1)]
                if c >= 2:
                    pe.wait_ge(q_used, c - 1)
                for j in range(2):
                    for k in range(KD):
                        if c == 0 and j == 0 and k % 2 == 0:
                            pe.wait_ge(ft_done, k // 2 + 1)
                        last = pe.matmul(ps[:, 4 + c % 2, j * T:(j + 1) * T], w[k // UK][:, k % UK, j * P:(j + 1) * P],
                                         fT[:, k, :], start=(k == 0), stop=(k == KD - 1))
                        if j == 1 and k == UK - 1:
                            last.then_inc(unit_done, 1)
                last.then_inc(q_full, 1)
                pe.wait_ge(q_used, c + 1)
                if c >= 2:
                    pe.wait_ge(sc_done, c - 1)
                for i in range(2):
                    for j in range(2):
                        last = pe.matmul(ps[:, 6 + c % 2, (2 * i + j) * P:(2 * i + j + 1) * P],
                                         qT[:, j, i * P:(i + 1) * P], skT[:, j], start=True, stop=True)
                last.then_inc(sc_full, 1)

            for c in range(EARLY_HEADS):
                query(c)
            pe.wait_ge(out_used, NCH)
            pe.wait_ge(ft_done, KD // 2)
            for m in range(NI * K):
                i, j = divmod(m, K)
                if j == K // 2 and EARLY_HEADS + i < HEADS:
                    query(EARLY_HEADS + i)
                if m == HEADS * K:
                    pe.wait_ge(sc_done, HEADS)
                tile, r = divmod(m, HEADS * K)
                pe.wait_ge(v_in[m % NV], 16 * (m // NV + 1))
                pe.wait_ge(diag_done, m + 1)
                for c in range(D // 512):
                    last = pe.matmul(ps[:, 4 * tile + c, :], diag[:, m % NDIAG], vb[m % NV][:, c * 512:(c + 1) * 512],
                                     start=(r == 0), stop=(r == HEADS * K - 1))
                last.then_inc(v_used, 1)


_INS = ['x', 'c', 'ctx', 'c_ctx', 'w_ada', 'b_ada', 'g_norm1', 'w_in', 's5_a_re', 's5_a_im', 's5_log_dt', 's5_b_re',
        's5_b_im', 's5_c_re', 's5_c_im', 's5_d', 's5_w_glu', 'lru_conv_w', 'lru_conv_b', 'lru_lambda', 'lru_w_r',
        'lru_b_r', 'lru_w_i', 'lru_b_i', 'w_proj_a', 'w_proj_b', 'w_out', 'g_norm2', 'peer_w_query',
        'peer_sub_keys', 'peer_u', 'peer_v', 'g_final']


def kernel(**inputs):
    import concourse.bacc as _bacc
    from concourse.bass_utils import run_bass_kernel_spmd as _run

    nc = _bacc.Bacc("TRN2", target_bir_lowering=False, num_devices=1)
    arrays, aps = {}, {}
    for name in _INS:
        a = np.ascontiguousarray(inputs[name])
        arrays[f"in_{name}"] = a
        aps[name] = nc.dram_tensor(f"in_{name}", a.shape, mybir.dt.from_np(a.dtype), kind="ExternalInput").ap()
    aps["out"] = nc.dram_tensor("out_0", (1, T, D), F32, kind="ExternalOutput").ap()
    build(nc, aps)
    r = _run(nc, [arrays], core_ids=[0])
    return r.results[0]["out_0"]
```
